# Optimizing a Trainium2 kernel written in Bass

```python
import math
import jax, jax.numpy as jnp
from jax import lax
import numpy as np

D_MODEL = 1024
BATCH = 1
SEQ = 256
DEPTH = 2

HEAD_DIM = 64
MOBA_HEADS = 4
MOBA_BLOCK = 256
MOBA_TOPK = 3
SWA_Q_HEADS = 4
SWA_KV_HEADS = 2
SWA_WINDOW = 128
DIFF_HEADS = 4
DIFF_V_DIM = 2 * HEAD_DIM
A_Q = MOBA_HEADS * HEAD_DIM
B_Q = SWA_Q_HEADS * HEAD_DIM
B_KV = SWA_KV_HEADS * HEAD_DIM
C_QK = DIFF_HEADS * 2 * HEAD_DIM
C_V = DIFF_HEADS * DIFF_V_DIM
N_BRANCH = 3
SPLIT_SIZES = (A_Q, A_Q, A_Q, B_Q, B_KV, B_KV, C_QK, C_QK, C_V, N_BRANCH * D_MODEL)
IN_COLS = A_Q * 3 + B_Q + 2 * B_KV + 2 * C_QK + C_V + N_BRANCH * D_MODEL
D_FF = 2816
FFN_HALF = 0.5
ROPE_THETA = 10000.0
Q_BLOCK = 128
EPS = 1e-6
NEG = -1e30

kernel_name = "hybrid_moba_swa_diff_macaron"

def rmsnorm(x, gain):
    xf = x.astype(jnp.float32)
    y = xf * lax.rsqrt(jnp.mean(xf * xf, axis=-1, keepdims=True) + EPS)
    return (y * gain.astype(jnp.float32)).astype(x.dtype)

def rope_tables(seq):
    pos = jnp.arange(seq, dtype=jnp.float32)
    inv_freq = ROPE_THETA ** (-jnp.arange(0, HEAD_DIM, 2, dtype=jnp.float32) / HEAD_DIM)
    ang = pos[:, None] * inv_freq[None, :]
    return jnp.cos(ang), jnp.sin(ang)

def apply_rope(x, cos, sin):
    xf = x.astype(jnp.float32)
    x1, x2 = jnp.split(xf, 2, axis=-1)
    out = jnp.concatenate([x1 * cos - x2 * sin, x2 * cos + x1 * sin], axis=-1)
    return out.astype(x.dtype)

def to_heads(t, n_heads, dim):
    b, s, _ = t.shape
    return t.reshape(b, s, n_heads, dim).transpose(0, 2, 1, 3)

def from_heads(t):
    b, h, s, d = t.shape
    return t.transpose(0, 2, 1, 3).reshape(b, s, h * d)

def qk_prep(t, gain, cos, sin):
    return apply_rope(rmsnorm(t, gain), cos, sin)

def swiglu(x, w_gate, w_up, w_down):
    return (jax.nn.silu(x @ w_gate) * (x @ w_up)) @ w_down

def moba_attention(q, k, v):
    b, h, s, dh = q.shape
    nb = -(-s // MOBA_BLOCK)
    pad = nb * MOBA_BLOCK - s
    kp = jnp.pad(k, ((0, 0), (0, 0), (0, pad), (0, 0)))
    vp = jnp.pad(v, ((0, 0), (0, 0), (0, pad), (0, 0)))
    kb = kp.reshape(b, h, nb, MOBA_BLOCK, dh)
    vb = vp.reshape(b, h, nb, MOBA_BLOCK, dh)
    kmean = jnp.mean(kb.astype(jnp.float32), axis=3)
    n_sel = min(MOBA_TOPK, nb - 1)
    scale = dh ** -0.5
    bi = jnp.arange(b)[:, None, None, None]
    hi = jnp.arange(h)[None, :, None, None]
    n_chunks = s // Q_BLOCK

    def chunk(c):
        start = c * Q_BLOCK
        qc = lax.dynamic_slice_in_dim(q, start, Q_BLOCK, axis=2)
        tq = start + jnp.arange(Q_BLOCK)
        cur = start // MOBA_BLOCK
        own_k = lax.dynamic_index_in_dim(kb, cur, axis=2, keepdims=False)
        own_v = lax.dynamic_index_in_dim(vb, cur, axis=2, keepdims=False)
        kpos = cur * MOBA_BLOCK + jnp.arange(MOBA_BLOCK)
        s_own = jnp.einsum('bhqd,bhkd->bhqk', qc, own_k, preferred_element_type=jnp.float32) * scale
        s_own = jnp.where(kpos[None, :] <= tq[:, None], s_own, NEG)
        if n_sel > 0:
            gate = jnp.einsum('bhqd,bhnd->bhqn', qc.astype(jnp.float32), kmean)
            past = jnp.arange(nb) < cur
            gate = jnp.where(past, gate, NEG)
            _, gidx = lax.top_k(gate, n_sel)
            valid = past[gidx]
            kg = kb[bi, hi, gidx]
            vg = vb[bi, hi, gidx]
            s_sel = jnp.einsum('bhqd,bhqnkd->bhqnk', qc, kg, preferred_element_type=jnp.float32) * scale
            s_sel = jnp.where(valid[..., None], s_sel, NEG)
            n_keys = n_sel * MOBA_BLOCK
            s_all = jnp.concatenate([s_sel.reshape(b, h, Q_BLOCK, n_keys), s_own], axis=-1)
            p = jax.nn.softmax(s_all, axis=-1).astype(v.dtype)
            p_sel = p[..., :n_keys].reshape(b, h, Q_BLOCK, n_sel, MOBA_BLOCK)
            p_own = p[..., n_keys:]
            return (jnp.einsum('bhqnk,bhqnkd->bhqd', p_sel, vg)
                    + jnp.einsum('bhqk,bhkd->bhqd', p_own, own_v))
        p_own = jax.nn.softmax(s_own, axis=-1).astype(v.dtype)
        return jnp.einsum('bhqk,bhkd->bhqd', p_own, own_v)

    outs = lax.map(chunk, jnp.arange(n_chunks))
    return outs.transpose(1, 2, 0, 3, 4).reshape(b, h, s, dh)

def sliding_window_sink_attention(q, k, v, sinks):
    b, hq, s, dh = q.shape
    hkv = k.shape[1]
    g = hq // hkv
    nc = s // Q_BLOCK
    scale = dh ** -0.5
    qb = q.reshape(b, hkv, g, nc, Q_BLOCK, dh)
    kb = k.reshape(b, hkv, nc, Q_BLOCK, dh)
    vb = v.reshape(b, hkv, nc, Q_BLOCK, dh)
    pad = ((0, 0), (0, 0), (1, 0), (0, 0), (0, 0))
    kband = jnp.concatenate([jnp.pad(kb, pad)[:, :, :-1], kb], axis=3)
    vband = jnp.concatenate([jnp.pad(vb, pad)[:, :, :-1], vb], axis=3)
    sc = jnp.einsum('bhgcqd,bhckd->bhgcqk', qb, kband, preferred_element_type=jnp.float32) * scale
    diff = (jnp.arange(Q_BLOCK)[:, None] + Q_BLOCK) - jnp.arange(2 * Q_BLOCK)[None, :]
    in_window = (diff >= 0) & (diff < SWA_WINDOW)
    kabs = (jnp.arange(nc)[:, None] - 1) * Q_BLOCK + jnp.arange(2 * Q_BLOCK)[None, :]
    mask = in_window[None] & (kabs >= 0)[:, None, :]
    sc = jnp.where(mask, sc, NEG)
    sink = sinks.astype(jnp.float32).reshape(hkv, g)[None, :, :, None, None, None]
    sink = jnp.broadcast_to(sink, sc.shape[:-1] + (1,))
    p = jax.nn.softmax(jnp.concatenate([sc, sink], axis=-1), axis=-1)[..., :-1]
    out = jnp.einsum('bhgcqk,bhckd->bhgcqd', p.astype(v.dtype), vband)
    return out.reshape(b, hq, s, dh)

def differential_attention(q1, q2, k1, k2, v, lam):
    b, h, s, dh = q1.shape
    nc = s // Q_BLOCK
    scale = dh ** -0.5
    kpos = jnp.arange(s)

    def chunk(c):
        start = c * Q_BLOCK
        causal = kpos[None, :] <= (start + jnp.arange(Q_BLOCK))[:, None]

        def attn_map(qq, kk):
            qc = lax.dynamic_slice_in_dim(qq, start, Q_BLOCK, axis=2)
            sc = jnp.einsum('bhqd,bhkd->bhqk', qc, kk, preferred_element_type=jnp.float32) * scale
            return jax.nn.softmax(jnp.where(causal, sc, NEG), axis=-1)

        a = attn_map(q1, k1) - lam * attn_map(q2, k2)
        return jnp.einsum('bhqk,bhkd->bhqd', a.astype(v.dtype), v)

    outs = lax.map(chunk, jnp.arange(nc))
    return outs.transpose(1, 2, 0, 3, 4).reshape(b, h, s, v.shape[-1])

def token_mixing(h, cos, sin, lam_init, w_in, moba_q_norm, moba_k_norm, swa_q_norm,
                 swa_k_norm, swa_sinks, diff_q_norm, diff_k_norm, lq1, lk1, lq2, lk2,
                 diff_subln, w_branch_a, w_branch_b, w_branch_c, w_out):
    b, s, _ = h.shape
    points = np.cumsum(SPLIT_SIZES)[:-1].tolist()
    proj = h @ w_in
    qa, ka, va, qb, kb, vb, qc, kc, vc, gate_logits = jnp.split(proj, points, axis=-1)
    qa = qk_prep(to_heads(qa, MOBA_HEADS, HEAD_DIM), moba_q_norm, cos, sin)
    ka = qk_prep(to_heads(ka, MOBA_HEADS, HEAD_DIM), moba_k_norm, cos, sin)
    va = to_heads(va, MOBA_HEADS, HEAD_DIM)
    ya = from_heads(moba_attention(qa, ka, va)) @ w_branch_a
    qb = qk_prep(to_heads(qb, SWA_Q_HEADS, HEAD_DIM), swa_q_norm, cos, sin)
    kb = qk_prep(to_heads(kb, SWA_KV_HEADS, HEAD_DIM), swa_k_norm, cos, sin)
    vb = to_heads(vb, SWA_KV_HEADS, HEAD_DIM)
    yb = from_heads(sliding_window_sink_attention(qb, kb, vb, swa_sinks)) @ w_branch_b
    q1, q2 = jnp.split(to_heads(qc, DIFF_HEADS, 2 * HEAD_DIM), 2, axis=-1)
    k1, k2 = jnp.split(to_heads(kc, DIFF_HEADS, 2 * HEAD_DIM), 2, axis=-1)
    q1 = qk_prep(q1, diff_q_norm, cos, sin)
    q2 = qk_prep(q2, diff_q_norm, cos, sin)
    k1 = qk_prep(k1, diff_k_norm, cos, sin)
    k2 = qk_prep(k2, diff_k_norm, cos, sin)
    vc = to_heads(vc, DIFF_HEADS, DIFF_V_DIM)
    f32 = jnp.float32
    lam = (jnp.exp(jnp.sum(lq1.astype(f32) * lk1.astype(f32)))
           - jnp.exp(jnp.sum(lq2.astype(f32) * lk2.astype(f32))) + lam_init)
    oc = differential_attention(q1, q2, k1, k2, vc, lam)
    oc = rmsnorm(oc, diff_subln) * (1.0 - lam_init)
    yc = from_heads(oc) @ w_branch_c
    gates = jax.nn.sigmoid(gate_logits.astype(f32)).astype(h.dtype).reshape(b, s, N_BRANCH, D_MODEL)
    merged = gates[:, :, 0] * ya + gates[:, :, 1] * yb + gates[:, :, 2] * yc
    return merged @ w_out

def setup_inputs(seed: int = 0) -> dict:
    key = jax.random.key(seed)
    ks = jax.random.split(key, 32)
    L, D, F, dh = DEPTH, D_MODEL, D_FF, HEAD_DIM

    def w(k, shape, fan_in):
        return jax.random.normal(k, shape, jnp.float32) * fan_in ** -0.5

    def gain(k, shape):
        return 1.0 + 0.02 * jax.random.normal(k, shape, jnp.float32)

    def small(k, shape, sc):
        return sc * jax.random.normal(k, shape, jnp.float32)

    return {
        "x": jax.random.normal(ks[0], (BATCH, SEQ, D), jnp.float32),
        "ffn1_norm": gain(ks[1], (L, D)),
        "ffn1_w_gate": w(ks[2], (L, D, F), D),
        "ffn1_w_up": w(ks[3], (L, D, F), D),
        "ffn1_w_down": w(ks[4], (L, F, D), F),
        "mix_norm": gain(ks[5], (L, D)),
        "w_in": w(ks[6], (L, D, IN_COLS), D),
        "moba_q_norm": gain(ks[7], (L, dh)),
        "moba_k_norm": gain(ks[8], (L, dh)),
        "swa_q_norm": gain(ks[9], (L, dh)),
        "swa_k_norm": gain(ks[10], (L, dh)),
        "swa_sinks": small(ks[11], (L, SWA_Q_HEADS), 0.5),
        "diff_q_norm": gain(ks[12], (L, dh)),
        "diff_k_norm": gain(ks[13], (L, dh)),
        "diff_lambda_q1": small(ks[14], (L, dh), 0.1),
        "diff_lambda_k1": small(ks[15], (L, dh), 0.1),
        "diff_lambda_q2": small(ks[16], (L, dh), 0.1),
        "diff_lambda_k2": small(ks[17], (L, dh), 0.1),
        "diff_subln": gain(ks[18], (L, DIFF_V_DIM)),
        "w_branch_a": w(ks[19], (L, A_Q, D), A_Q),
        "w_branch_b": w(ks[20], (L, B_Q, D), B_Q),
        "w_branch_c": w(ks[21], (L, C_V, D), C_V),
        "w_out": w(ks[22], (L, D, D), D),
        "ffn2_norm": gain(ks[23], (L, D)),
        "ffn2_w_gate": w(ks[24], (L, D, F), D),
        "ffn2_w_up": w(ks[25], (L, D, F), D),
        "ffn2_w_down": w(ks[26], (L, F, D), F),
    }

def reference(x, ffn1_norm, ffn1_w_gate, ffn1_w_up, ffn1_w_down, mix_norm, w_in,
              moba_q_norm, moba_k_norm, swa_q_norm, swa_k_norm, swa_sinks,
              diff_q_norm, diff_k_norm, diff_lambda_q1, diff_lambda_k1,
              diff_lambda_q2, diff_lambda_k2, diff_subln, w_branch_a, w_branch_b,
              w_branch_c, w_out, ffn2_norm, ffn2_w_gate, ffn2_w_up, ffn2_w_down):
    cos, sin = rope_tables(x.shape[1])
    for l in range(DEPTH):
        lam_init = 0.8 - 0.6 * math.exp(-0.3 * l)
        x = x + FFN_HALF * swiglu(rmsnorm(x, ffn1_norm[l]), ffn1_w_gate[l], ffn1_w_up[l], ffn1_w_down[l])
        x = x + token_mixing(rmsnorm(x, mix_norm[l]), cos, sin, lam_init, w_in[l],
                             moba_q_norm[l], moba_k_norm[l], swa_q_norm[l], swa_k_norm[l],
                             swa_sinks[l], diff_q_norm[l], diff_k_norm[l],
                             diff_lambda_q1[l], diff_lambda_k1[l], diff_lambda_q2[l],
                             diff_lambda_k2[l], diff_subln[l], w_branch_a[l], w_branch_b[l],
                             w_branch_c[l], w_out[l])
        x = x + FFN_HALF * swiglu(rmsnorm(x, ffn2_norm[l]), ffn2_w_gate[l], ffn2_w_up[l], ffn2_w_down[l])
    return x


_drawn_inputs = setup_inputs


def setup_inputs(seed=0):
    import zlib

    import numpy as np

    out = dict(_drawn_inputs(seed))
    spreads = {}
    factors = {'ffn1_norm': 3.959,
     'moba_q_norm': 8.0,
     'moba_k_norm': 8.0,
     'swa_q_norm': 8.0,
     'swa_k_norm': 8.0,
     'swa_sinks': 200.0,
     'diff_q_norm': 5.961,
     'diff_k_norm': 5.378,
     'diff_subln': 14.348,
     'ffn2_norm': 5.393}
    for name, (base, spread) in spreads.items():
        noise = np.random.default_rng([zlib.crc32(name.encode()), seed]).standard_normal(out[name].shape)
        drawn = base * np.exp(spread * noise) if base else spread * noise
        out[name] = __import__('jax').numpy.asarray(drawn.astype(out[name].dtype))
    for name, factor in factors.items():
        out[name] = (out[name] * factor).astype(out[name].dtype)
    return out
```

```python
from contextlib import ExitStack

import numpy as np

import concourse.bass as bass
from concourse import mybir

F32 = mybir.dt.float32
F32R = mybir.dt.float32r
I32 = mybir.dt.int32
ALU = mybir.AluOpType
ACT = mybir.ActivationFunctionType
AXIS_X = mybir.AxisListType.X

P = 128
S = 256
HALVES = S // P
D = 1024
KB = D // P
F = 2816
FC = 256
CHUNKS = F // FC
DH = 64
DEPTH = 2
EPS = 1e-6
NEG = -1e30
SCALE = DH ** -0.5
LAM_INIT = [0.8 - 0.6 * float(np.exp(-0.3 * layer)) for layer in range(DEPTH)]

QA, KA, VA, QB, KBC, VB, QC, KC, VC, GATES = 0, 256, 512, 768, 1024, 1152, 1280, 1792, 2304, 2816
PROJ = [(QC, 512), (KC, 512), (VC, 512), (QA, 512), (VA, 512), (KBC, 256)] + [(GATES + 512 * g, 512) for g in range(6)]

RING = 6
FFN_PAIRS = CHUNKS * 6
PROJ_PAIRS = sum(width // 128 for _, width in PROJ)
BRANCH_PAIRS = KB
OUT_PAIRS = KB
MIX0 = FFN_PAIRS
BRANCH0 = MIX0 + PROJ_PAIRS
OUT0 = BRANCH0 + BRANCH_PAIRS
FFN2_0 = OUT0 + OUT_PAIRS
PAIRS = FFN2_0 + FFN_PAIRS
FILLS = PAIRS // 2

G_FFN1, G_MIX, G_FFN2, G_SUBLN = 0, 8, 16, 24
SINK, NEG_LAM, ROPE_GAIN = 25, 29, 30
PARAMS = ROPE_GAIN + 6 * DH
GAIN_ROWS = (3 * KB + 1) * DEPTH
ST_FFN1, ST_MIX, ST_O, ST_MERGED, ST_FFN2 = range(5)

UNITS = [("C", h, 4 + h, 15 + 3 * h) for h in range(4)] + [("A", 8 + j, 10 + j, 27 + 3 * j) for j in range(2)] \
    + [("B", 12 + j, 14, 33 + 3 * j) for j in range(2)]
ROPE_TURNS = [(0, 4, 9), (4, 4, 13), (8, 4, 23), (12, 3, 32)]
O_TURNS = [38, 43]

PER_LAYER = {
    "pair_used": PAIRS, "high_ready": PAIRS, "low_ready": PAIRS,
    "blocks_turned": 10, "blocks_high": 20, "blocks_low": 20,
    "gate_up_done": 2 * CHUNKS, "silu_ready": 2 * CHUNKS * HALVES, "hidden_ready": 2 * CHUNKS,
    "hidden_turned": 2 * CHUNKS, "hidden_high": 2 * CHUNKS, "hidden_low": 2 * CHUNKS,
    "product_done": 18, "residual_done": 12, "merged": 12,
    "squares_ready": 3, "norm_ready": 3, "params_ready": 1,
    "proj_done": len(PROJ), "proj_read": len(PROJ), "head_squares": 5, "rope_done": 5,
    "rope_turned": 4, "rope_copied": 4,
    "scores_done": 8, "scores_masked": 8, "exps_ready": 8, "probs_ready": 8, "probs_turned": 8,
    "probs_copied": 8, "context_done": 8, "context_read": 8, "subln_squares": 1, "subln_ready": 1,
}
CREDIT = {"pair_used": RING, "low_ready": 2 * RING, "residual_done": 4}


def ring_slots(items, mix_first, mix_items):
    full_rounds = next(a for a in range(mix_items // RING, -1, -1)
                       if (mix_items - RING * a) % (RING - 1) == 0)
    short_rounds = (mix_items - RING * full_rounds) // (RING - 1)
    slots = [n % RING for n in range(mix_first)]
    first = mix_first % RING
    order = [(first + k) % RING for k in range(RING)]
    slots += order[:-1] * short_rounds + order * full_rounds
    slots += [(first + k) % RING for k in range(items - len(slots))]
    assert slots[-1] == RING - 1
    return slots


def earlier(slots):
    return [max(m for m in range(n - len(slots), n) if slots[m] == slots[n]) for n in range(len(slots))]


FILL_SLOT = ring_slots(FILLS, MIX0 // 2, (FFN2_0 - MIX0) // 2)
PAIR_SLOT = ring_slots(PAIRS, MIX0, FFN2_0 - MIX0)
FILL_BEFORE, PAIR_BEFORE = earlier(FILL_SLOT), earlier(PAIR_SLOT)


def build(nc, a):
    ctx = ExitStack()
    with ctx:
        def sb(name, shape, dt=F32):
            return ctx.enter_context(nc.sbuf_tensor(name, shape, dt))

        raw = sb("raw", [P, RING, 2048])
        w_high = sb("w_high", [P, RING, 1024], F32R)
        w_low = sb("w_low", [P, RING, 1024], F32R)
        x = sb("x", [P, HALVES, D])
        xT_high = sb("xT_high", [P, KB, S], F32R)
        xT_low = sb("xT_low", [P, KB, S], F32R)
        oT_high = sb("oT_high", [P, KB, S], F32R)
        oT_low = sb("oT_low", [P, KB, S], F32R)
        gates = sb("gates", [P, HALVES, 3 * D])
        values = sb("values", [P, HALVES, 896])
        o_nat = sb("o_nat", [P, HALVES, D])
        work = sb("work", [P, 2048])
        silu = work[:, 0:512].rearrange("p (t f) -> p t f", t=HALVES)
        hidden = work[:, 512:1024].rearrange("p (t f) -> p t f", t=HALVES)
        hT_high = sb("hT_high", [P, 2, S], F32R)
        hT_low = sb("hT_low", [P, 2, S], F32R)
        qk_raw = [work[:, 1024 * b:1024 * b + 1024].rearrange("p (t c) -> p t c", t=HALVES) for b in range(2)]
        merged = work[:, :].rearrange("p (t c) -> p t c", t=HALVES)
        roped = o_nat[:, :, 0:512]
        scratch = sb("scratch", [P, HALVES, 512])
        probs = sb("probs", [P, 2, 384])
        probsT = sb("probsT", [P, 2, 384])
        ident = sb("ident", [P, P])
        masks = sb("masks", [P, 4, P])
        zero = sb("zero", [P, P], F32R)
        trig = sb("trig", [P, 2, HALVES, DH])
        params_all = sb("params_all", [P, DEPTH, PARAMS])
        params = sb("params", [P, PARAMS])
        rope_cos, rope_sin = (gates[:, n, 4 * 512:4 * 512 + 12 * DH].rearrange("p (i t d) -> p i t d", i=6, t=HALVES) for n in range(2))
        lam_vec = probs[:, :, :].rearrange("p a b -> p (a b)")[:, 0:4 * DEPTH * DH].rearrange("p (i l d) -> p i l d", i=4, l=DEPTH)
        gain_rows = probsT[:, 0, 0:P]
        small = sb("small", [P, 8, 16])
        head_scale = sb("head_scale", [P, HALVES, 30])
        norm_sq = sb("norm_sq", [P, HALVES])
        norm_scale = sb("norm_scale", [P, HALVES])
        row_max = sb("row_max", [P, 4])
        neg_max = sb("neg_max", [P, 4])
        row_sum = sb("row_sum", [P, 4])
        inv_sum = sb("inv_sum", [P, 4])
        sink_diff = sb("sink_diff", [P, 4])
        sink_exp = sb("sink_exp", [P, 4])
        bank = [ctx.enter_context(nc.psum_tensor(f"bank{b}", [P, 512], F32)) for b in range(8)]

        sem = {name: ctx.enter_context(nc.semaphore(name)) for name in PER_LAYER}
        fill_landed = [ctx.enter_context(nc.semaphore(f"fill_landed{n}")) for n in range(RING)]
        x_loaded = ctx.enter_context(nc.semaphore("x_loaded"))
        rows_loaded = ctx.enter_context(nc.semaphore("rows_loaded"))
        params_loaded = ctx.enter_context(nc.semaphore("params_loaded"))
        constants_ready = ctx.enter_context(nc.semaphore("constants_ready"))
        gains_turned = ctx.enter_context(nc.semaphore("gains_turned"))
        lambda_sums = ctx.enter_context(nc.semaphore("lambda_sums"))
        lambda_exps = ctx.enter_context(nc.semaphore("lambda_exps"))
        fills_started = ctx.enter_context(nc.semaphore("fills_started"))
        units_started = ctx.enter_context(nc.semaphore("units_started"))
        stored = ctx.enter_context(nc.semaphore("stored"))
        block = ctx.enter_context(nc.Block())

        def qk_blocks(first, count):
            base, per_half, c0 = (0, 4, 0) if first < 8 else (8, 2, 1024) if first < 12 else (12, 2, 1536)
            half, n = divmod(first - base, per_half)
            return gates[:, half, c0 + n * S:c0 + (n + count) * S]

        GROUP_BANKS = {ST_FFN1: (2, 3), ST_MIX: (2, 3), ST_O: (6, 7), ST_MERGED: (2, 3), ST_FFN2: (2, 3)}
        QUARTERS = [(0, 0), (1, 0), (0, 1), (1, 1)]

        def quarter(half, cols):
            return bank[4 + half + 2 * cols]

        def group_blocks(stage, group):
            first = 4 * (1 - group) if stage == ST_O else 4 * group
            return range(first, first + 4)

        def stage_tiles(stage):
            return (oT_high, oT_low) if stage == ST_O else (xT_high, xT_low)

        def banks_split(stage, group, n):
            return 4 * stage + 2 * group + n + 1

        def value(name, layer, k):
            return layer * PER_LAYER[name] + (k + CREDIT.get(name, 0))

        @block.sync
        def _(sp):
            def fill(layer, n, sources, n_reg=None):
                slot = FILL_SLOT[n]
                sp.wait_ge(sem["low_ready"], value("low_ready", layer, (0 if n_reg is None else n_reg) + 2 * FILL_BEFORE[n] + 2))
                sp.sem_inc(fills_started, 1)
                for dst, src in sources(raw[:, slot]):
                    sp.dma_start(dst, src).then_inc(fill_landed[slot], 16)

            def rows(w, layer, k0, nk, c0, width):
                return w[bass.ds(layer, 1), k0 * P:(k0 + nk) * P, c0:c0 + width].rearrange("o (k p) c -> p (o k) c", p=P)

            def gate_up(wg, wu, layer, c, k0):
                def sources(slot):
                    v = slot.rearrange("p (k g c) -> p k g c", k=4, g=2)
                    for g, w in enumerate((wg, wu)):
                        yield v[:, :, g], w[bass.ds(layer, 1), k0 * P:(k0 + 4) * P, bass.ds(c * FC, FC)].rearrange(
                            "o (k p) c -> p (o k) c", p=P)
                return sources

            def down(wd, layer, c):
                def sources(slot):
                    v = slot.rearrange("p (k c) -> p k c", k=2)
                    for k in range(2):
                        yield v[:, k], wd[bass.ds(layer, 1), bass.ds(c * FC + k * P, P), :].rearrange("o p c -> p (o c)")
                return sources

            def wide(w, layer, k0):
                def sources(slot):
                    v = slot.rearrange("p (k c) -> p k c", k=2)
                    for k in range(2):
                        yield v[:, k], w[bass.ds(layer, 1), (k0 + k) * P:(k0 + k + 1) * P, :].rearrange("o p c -> p (o c)")
                return sources

            def proj(layer, c0, width, k0, nk):
                def sources(slot):
                    v = slot.rearrange("p (k c) -> p k c", k=nk)
                    for h in range(2):
                        yield v[:, h * nk // 2:(h + 1) * nk // 2], rows(a["w_in"], layer, k0 + h * nk // 2, nk // 2, c0, width)
                return sources

            def ffn(layer, first, wg, wu, wd):
                n = first // 2
                fill(layer, n, gate_up(wg, wu, layer, 0, 0))
                fill(layer, n + 1, gate_up(wg, wu, layer, 0, 4))
                with sp.Fori(0, (CHUNKS - 1) // 2) as i:
                    for j in range(2):
                        m = n + 2 + 3 * j
                        fill(layer, m, gate_up(wg, wu, layer, 2 * i + (j + 1), 0), i * 12)
                        fill(layer, m + 1, gate_up(wg, wu, layer, 2 * i + (j + 1), 4), i * 12)
                        fill(layer, m + 2, down(wd, layer, 2 * i + j), i * 12)
                fill(layer, n + FFN_PAIRS // 2 - 1, down(wd, layer, CHUNKS - 1))

            sp.dma_start(x[:, 0], a["x"][0, 0:P, :]).then_inc(x_loaded, 16)
            sp.dma_start(x[:, 1], a["x"][0, P:S, :]).then_inc(x_loaded, 16)
            with sp.Fori(0, DEPTH) as layer:
                ffn(layer, 0, a["ffn1_w_gate"], a["ffn1_w_up"], a["ffn1_w_down"])
                n = MIX0 // 2
                for c0, width in PROJ:
                    if width == 512:
                        fill(layer, n, proj(layer, c0, width, 0, 4))
                        fill(layer, n + 1, proj(layer, c0, width, 4, 4))
                        n += 2
                    else:
                        fill(layer, n, proj(layer, c0, width, 0, 8))
                        n += 1
                for w, k0 in ((a["w_branch_c"], 0), (a["w_branch_c"], 2), (a["w_branch_a"], 0), (a["w_branch_b"], 0),
                              (a["w_out"], 0), (a["w_out"], 2), (a["w_out"], 4), (a["w_out"], 6)):
                    fill(layer, n, wide(w, layer, k0))
                    n += 1
                ffn(layer, FFN2_0, a["ffn2_w_gate"], a["ffn2_w_up"], a["ffn2_w_down"])
            sp.wait_ge(sem["residual_done"], CREDIT["residual_done"] + DEPTH * PER_LAYER["residual_done"])
            sp.dma_start(a["out"][0].rearrange("(t p) d -> p t d", p=P), x[:, :, :]).then_inc(stored, 16)
            sp.wait_ge(stored, 16)

        @block.gpsimd
        def _(pool):
            pool.memset(ident[:, :], 0.0)
            pool.memset(masks[:, :, :], 0.0)
            pool.memset(zero[:, :].bitcast(F32), 0.0)
            pool.drain()
            pool.affine_select(out=ident[:, :], in_=ident[:, :], compare_op=ALU.not_equal, fill=1.0, base=0,
                               pattern=[[-1, P]], channel_multiplier=1)
            for n in (1, 3):
                pool.affine_select(out=masks[:, n], in_=masks[:, n], compare_op=ALU.is_ge, fill=NEG, base=0,
                                   pattern=[[-1, P]], channel_multiplier=1)
            pool.affine_select(out=masks[:, 2], in_=masks[:, 2], compare_op=ALU.is_gt, fill=NEG, base=0,
                               pattern=[[1, P]], channel_multiplier=-1)
            pool.drain().then_inc(constants_ready, 1)

        @block.tensor
        def _(pe):
            def three_passes(out, left_high, left_low, slot, cols, start, stop, release=0):
                first = nc.tensor.matmul(out, left_high, w_high[:, slot, cols], start=start, stop=False)
                if release:
                    first.then_inc(sem["pair_used"], release)
                nc.tensor.matmul(out, left_low, w_high[:, slot, cols], start=False, stop=False)
                return nc.tensor.matmul(out, left_high, w_low[:, slot, cols], start=False, stop=stop)

            def token(tile, kb, half):
                return tile[:, kb, half * P:(half + 1) * P]

            def turn_group(layer, stage, group, source):
                blocks = group_blocks(stage, group)
                for n, kb in enumerate(blocks):
                    for half in range(HALVES):
                        last = nc.tensor.transpose(
                            bank[GROUP_BANKS[stage][n // 2]][:, (n % 2) * S + half * P:(n % 2) * S + half * P + P],
                            source[:, half, kb * P:(kb + 1) * P], ident[:, :])
                last.then_inc(sem["blocks_turned"], 1)

            def gate_up_pair(layer, p, j, i_pairs=0, release=0):
                pe.wait_ge(sem["low_ready"], value("low_ready", layer, i_pairs + p + 1))
                for k in (2 * j, 2 * j + 1):
                    for half in range(HALVES):
                        last = three_passes(bank[half][:, :], token(xT_high, k, half), token(xT_low, k, half), PAIR_SLOT[p],
                                            slice((k % 2) * 512, (k % 2) * 512 + 512), k == 0, k == KB - 1, release)
                        release = 0
                last.then_inc(sem["gate_up_done" if j == 3 else "pair_used"], 1)

            def wide_pair(layer, p, high, low, kb, start, i_pairs=0, release=0):
                pe.wait_ge(sem["low_ready"], value("low_ready", layer, i_pairs + p + 1))
                for half, cols in QUARTERS:
                    last = three_passes(quarter(half, cols)[:, :], token(high, kb, half), token(low, kb, half), PAIR_SLOT[p],
                                        slice(cols * 512, cols * 512 + 512), start, False, release)
                    release = 0
                last.then_inc(sem["pair_used"], 1)

            def last_pairs(layer, p, high, low, kb, start, before_last=None, before=None, release=0):
                pe.wait_ge(sem["low_ready"], value("low_ready", layer, p + 2))
                for n, (half, cols) in enumerate(QUARTERS):
                    if before:
                        before(n)
                    if n == 3 and before_last:
                        before_last()
                    for k in range(2):
                        last = three_passes(quarter(half, cols)[:, :], token(high, kb + k, half), token(low, kb + k, half),
                                            PAIR_SLOT[p + k], slice(cols * 512, cols * 512 + 512), start and k == 0, k == 1,
                                            release)
                        release = 0
                    last.then_inc(sem["product_done"], 1)

            def turn_hidden(layer, chunk):
                pe.wait_ge(sem["hidden_ready"], value("hidden_ready", layer, chunk))
                for fb in range(2):
                    for half in range(HALVES):
                        last = nc.tensor.transpose(bank[2][:, fb * S + half * P:fb * S + half * P + P],
                                                   hidden[:, half, fb * P:(fb + 1) * P], ident[:, :])
                last.then_inc(sem["hidden_turned"], 1)

            def open_quarter(n):
                return nc.tensor.matmul(quarter(*QUARTERS[n])[:, :].rearrange("p (a b) -> p a b", a=4), zero[:, :],
                                        zero[:, :].unsqueeze(1).to_broadcast([P, 4, P]), start=True, stop=False)

            def ffn(layer, first, stage, turned, chunks_before, after):
                if not turned:
                    pe.wait_ge(sem["residual_done"], value("residual_done", layer, 0))
                    turn_group(layer, stage, 0, x)
                pe.wait_ge(sem["blocks_low"], value("blocks_low", layer, banks_split(stage, 0, 0)))
                gate_up_pair(layer, first, 0, release=2 if turned else 0)
                pe.wait_ge(sem["residual_done"], value("residual_done", layer, 0 if stage == ST_FFN1 else 8))
                pe.wait_ge(sem["blocks_low"], value("blocks_low", layer, banks_split(stage, 0, 1)))
                turn_group(layer, stage, 1, x)
                for n in range(3):
                    open_quarter(n)
                gate_up_pair(layer, first + 1, 1)
                pe.wait_ge(sem["blocks_low"], value("blocks_low", layer, banks_split(stage, 1, 0)))
                gate_up_pair(layer, first + 2, 2)
                pe.wait_ge(sem["blocks_low"], value("blocks_low", layer, banks_split(stage, 1, 1)))
                gate_up_pair(layer, first + 3, 3)
                open_quarter(3).then_inc(sem["pair_used"], 1)
                with pe.Fori(0, (CHUNKS - 1) // 2) as i:
                    for j in range(2):
                        p = first + 4 + 6 * j
                        done = i * 2 + (chunks_before + 1 + j)
                        turn_hidden(layer, done)
                        for n in range(4):
                            gate_up_pair(layer, p + n, n, i * 12)
                        pe.wait_ge(sem["hidden_low"], value("hidden_low", layer, done))
                        for n in range(2):
                            wide_pair(layer, p + 4 + n, hT_high, hT_low, n, False, i * 12, release=1 - n)
                done = chunks_before + CHUNKS
                turn_hidden(layer, done)
                pe.wait_ge(sem["hidden_low"], value("hidden_low", layer, done))
                last_pairs(layer, first + FFN_PAIRS - 2, hT_high, hT_low, 0, False, after)
                if after is None:
                    nc.tensor.matmul(bank[0][:, 0:P], zero[:, :], zero[:, :], start=True, stop=True).then_inc(sem["pair_used"], 2)

            def proj_pair(layer, chunk, j, release):
                p = MIX0 + sum(width // 128 for _, width in PROJ[:chunk]) + j
                width = PROJ[chunk][1]
                per_pair = 1024 // width
                pe.wait_ge(sem["low_ready"], value("low_ready", layer, p + 1))
                for n in range(per_pair):
                    k = j * per_pair + n
                    for half in range(HALVES):
                        last = three_passes(bank[2 * (chunk % 2) + half][:, 0:width], token(xT_high, k, half),
                                            token(xT_low, k, half), PAIR_SLOT[p], slice(n * width, (n + 1) * width),
                                            k == 0, k == KB - 1, release)
                        release = 0
                last.then_inc(sem["proj_done" if k == KB - 1 else "pair_used"], 1)

            def rope_turn(layer, n):
                first, count, _ = ROPE_TURNS[n]
                pe.wait_ge(sem["rope_done"], value("rope_done", layer, (1, 2, 3, 5)[n]))
                if n > 0:
                    pe.wait_ge(sem["rope_copied"], value("rope_copied", layer, n))
                if n >= 2:
                    pe.wait_ge(sem["context_read"], value("context_read", layer, {2: 2, 3: 5}[n]))
                for b in range(count):
                    for half in range(HALVES):
                        last = nc.tensor.transpose(bank[6 + b // 2][:, (b % 2) * S + half * P:(b % 2) * S + half * P + P],
                                                   roped[:, half, (b + (n == 3)) * P:(b + (n == 3) + 1) * P], ident[:, :])
                last.then_inc(sem["rope_turned"], 1)

            def scores(layer, u):
                kind, qb, kb, _ = UNITS[u]
                pe.wait_ge(sem["rope_copied"], value("rope_copied", layer, {"C": 2, "A": 3, "B": 4}[kind]))
                if u > 0:
                    pe.wait_ge(sem["scores_masked"], value("scores_masked", layer, u))
                else:
                    pe.wait_ge(sem["residual_done"], value("residual_done", layer, 4))
                q32, k32 = qk_blocks(qb, 1), qk_blocks(kb, 1)
                for t in range(2):
                    rows = slice(DH * t, DH * t + DH)
                    nc.tensor.matmul(bank[4 + t][:, 0:P], q32[rows, 0:P], k32[rows, 0:P], start=True, stop=True)
                    last = nc.tensor.matmul(bank[4 + t][:, P:3 * P], q32[rows, P:S], k32[rows, :], start=True, stop=True)
                last.then_inc(sem["scores_done"], 1)

            def turn_probs(layer, u):
                kind = UNITS[u][0]
                pe.wait_ge(sem["probs_ready"], value("probs_ready", layer, u + 1))
                if u > 0:
                    pe.wait_ge(sem["context_read"], value("context_read", layer, u))
                if u == 7:
                    pe.wait_ge(sem["blocks_low"], value("blocks_low", layer, banks_split(ST_O, 0, 1)))
                pe.wait_ge(sem["rope_copied"], value("rope_copied", layer, sum(pos <= UNITS[u][3] + 3 for _, _, pos in ROPE_TURNS)))
                for t in range(1 if kind == "C" else 2):
                    for b in range(3):
                        last = nc.tensor.transpose(bank[6 + t][:, b * P:(b + 1) * P], probs[:, t, b * P:(b + 1) * P], ident[:, :])
                last.then_inc(sem["probs_turned"], 1)

            def context(layer, u):
                kind = UNITS[u][0]
                pe.wait_ge(sem["probs_copied"], value("probs_copied", layer, u + 1))
                for t in range(1 if kind == "C" else 2):
                    if kind == "C":
                        out, c0, dv = bank[7][:, 0:S], 384 + u * P, P
                    else:
                        out, dv = bank[6 + t][:, 384:512], DH
                        c0 = (2 * (u - 4) + t) * DH if kind == "A" else 256 + t * DH
                    pT, v = probsT[:, t], values[:, :, c0:c0 + dv]
                    nc.tensor.matmul(out[:, 0:dv], pT[:, 0:P], v[:, 0], start=True, stop=True)
                    nc.tensor.matmul(out[:, dv:2 * dv], pT[:, P:2 * P], v[:, 0], start=True, stop=False)
                    last = nc.tensor.matmul(out[:, dv:2 * dv], pT[:, 2 * P:3 * P], v[:, 1], start=False, stop=True)
                last.then_inc(sem["context_done"], 1)

            def mixing(layer):
                chunk, j = 0, 0
                for m in range(PROJ_PAIRS):
                    if m == 1:
                        pe.wait_ge(sem["residual_done"], value("residual_done", layer, 4))
                        pe.wait_ge(sem["blocks_low"], value("blocks_low", layer, banks_split(ST_MIX, 0, 1)))
                        turn_group(layer, ST_MIX, 1, x)
                    if m in (0, 1):
                        pe.wait_ge(sem["blocks_low"], value("blocks_low", layer, banks_split(ST_MIX, 0, m)))
                    if m in (2, 3):
                        pe.wait_ge(sem["blocks_low"], value("blocks_low", layer, banks_split(ST_MIX, 1, m - 2)))
                    for u, (_, _, _, pos) in enumerate(UNITS):
                        if m == pos:
                            scores(layer, u)
                    for u, (_, _, _, pos) in enumerate(UNITS):
                        if m == pos + 3:
                            turn_probs(layer, u)
                        if m == pos + 4:
                            context(layer, u)
                    for n, (_, _, pos) in enumerate(ROPE_TURNS):
                        if m == pos:
                            rope_turn(layer, n)
                    if m in O_TURNS:
                        group = O_TURNS.index(m)
                        if group == 0:
                            pe.wait_ge(sem["subln_ready"], value("subln_ready", layer, 1))
                            pe.wait_ge(sem["context_read"], value("context_read", layer, 7))
                        else:
                            pe.wait_ge(sem["context_read"], value("context_read", layer, 8))
                            pe.wait_ge(sem["blocks_low"], value("blocks_low", layer, banks_split(ST_O, 0, 1)))
                        turn_group(layer, ST_O, group, o_nat)
                    if j == 0 and chunk >= 2:
                        pe.wait_ge(sem["proj_read"], value("proj_read", layer, chunk - 1))
                    if j == 0 and chunk == 1:
                        pe.wait_ge(sem["blocks_low"], value("blocks_low", layer, banks_split(ST_MIX, 1, 1)))
                    proj_pair(layer, chunk, j, release=0 if j else 1 if chunk else 2)
                    j += 1
                    if j == PROJ[chunk][1] // 128:
                        chunk, j = chunk + 1, 0

            def branches(layer):
                p = BRANCH0
                pe.wait_ge(sem["scores_masked"], value("scores_masked", layer, 8))
                pe.wait_ge(sem["blocks_low"], value("blocks_low", layer, banks_split(ST_O, 1, 1)))
                for k in range(4):
                    pe.wait_ge(sem["low_ready"], value("low_ready", layer, p + k + 1))
                    for n, (half, cols) in enumerate(QUARTERS):
                        last = three_passes(quarter(half, cols)[:, :], token(oT_high, 4 + k, half), token(oT_low, 4 + k, half),
                                            PAIR_SLOT[p + k], slice(cols * 512, cols * 512 + 512), k == 0, k == 3,
                                            release=1 if (k, n) == (0, 0) else 0)
                    last.then_inc(sem["product_done" if k == 3 else "pair_used"], 1)
                pe.wait_ge(sem["proj_read"], value("proj_read", layer, len(PROJ)))
                for k in range(2):
                    pe.wait_ge(sem["low_ready"], value("low_ready", layer, p + 4 + k + 1))
                    for n, (half, cols) in enumerate(QUARTERS):
                        last = three_passes(bank[half + 2 * cols][:, :], token(oT_high, k, half), token(oT_low, k, half),
                                            PAIR_SLOT[p + 4 + k], slice(cols * 512, cols * 512 + 512), k == 0, k == 1,
                                            release=1 if (k, n) == (0, 0) else 0)
                    last.then_inc(sem["product_done" if k == 1 else "pair_used"], 1)

                def quarter_free(n):
                    pe.wait_ge(sem["merged"], value("merged", layer, n + 1))

                def turn_merged():
                    pe.wait_ge(sem["merged"], value("merged", layer, 10))
                    turn_group(layer, ST_MERGED, 0, merged)

                last_pairs(layer, p + 6, oT_high, oT_low, 2, True, turn_merged, quarter_free, release=1)
                p = OUT0
                for k in range(KB - 2):
                    if k % 2 == 0:
                        pe.wait_ge(sem["blocks_low"], value("blocks_low", layer, banks_split(ST_MERGED, k // 4, k % 4 // 2)))
                    if k == 0:
                        pe.wait_ge(sem["merged"], value("merged", layer, 12))
                    if k == 1:
                        pe.wait_ge(sem["blocks_low"], value("blocks_low", layer, banks_split(ST_MERGED, 0, 1)))
                        turn_group(layer, ST_MERGED, 1, merged)
                    wide_pair(layer, p + k, xT_high, xT_low, k, k == 0, release=2 if k == 0 else 0)
                pe.wait_ge(sem["blocks_low"], value("blocks_low", layer, banks_split(ST_MERGED, 1, 1)))

                def turn_residual():
                    pe.wait_ge(sem["residual_done"], value("residual_done", layer, 6))
                    turn_group(layer, ST_FFN2, 0, x)

                last_pairs(layer, p + KB - 2, xT_high, xT_low, KB - 2, False, turn_residual)

            pe.wait_ge(constants_ready, 1)
            pe.wait_ge(rows_loaded, 16 * 4)
            nc.tensor.transpose(bank[0][:, 0:GAIN_ROWS], gain_rows[0:GAIN_ROWS, :], ident[0:GAIN_ROWS, 0:GAIN_ROWS]
                                ).then_inc(gains_turned, 1)
            pe.sem_inc(sem["pair_used"], CREDIT["pair_used"])
            with pe.Fori(0, DEPTH) as layer:
                def turn_for_mixing():
                    pe.wait_ge(sem["residual_done"], value("residual_done", layer, 2))
                    turn_group(layer, ST_MIX, 0, x)

                ffn(layer, 0, ST_FFN1, False, 0, turn_for_mixing)
                mixing(layer)
                branches(layer)
                ffn(layer, FFN2_0, ST_FFN2, True, CHUNKS, None)

        PROJ_END = np.cumsum([width // 128 for _, width in PROJ]) - 1
        ROPE_CHUNKS = {0: 1, 1: 2, 3: 3, 4: 4, 5: 5}
        SQUARES_AT = {0: 9, 1: 13, 3: 21, 4: 25, 5: 30}
        ROPE_AT = {0: 10, 1: 14, 3: 22, 4: 29, 5: 31}
        SIGMOID_AT = {6: 44, 7: 45, 8: 46}
        SUBLN_AT = 33
        MERGE_C_AT, MERGE_A_AT, MERGE_B_AT = 55, 57, 58
        ROPE_HEADS = {0: (0, 8, 0, [(0, 8, True)]), 1: (1, 8, 8, [(1, 8, False)]), 3: (0, 8, 16, [(2, 4, True), (3, 4, False)]),
                      4: (1, 4, 24, [(4, 4, True)]), 5: (0, 2, 28, [(5, 2, False)])}

        def query_scale(u, t, half):
            kind, h = UNITS[u][0], None
            h = {"C": 2 * u + t, "A": 16 + 2 * (u - 4) + t, "B": 24 + (u - 6) + 2 * t}[kind]
            return head_scale[:, half, h:h + 1]

        def context_column(u, t):
            return {"C": 512 + P * u, "A": (2 * (u - 4) + t) * DH, "B": 256 + (u - 6 + 2 * t) * DH}[UNITS[u][0]]

        @block.scalar
        def _(act):
            def high(layer, p, p_reg=None, fills=0):
                n, slot = p // 2, PAIR_SLOT[p]
                reg = 0 if p_reg is None else p_reg
                in_slot = FILL_SLOT[n]
                act.wait_ge(fill_landed[in_slot], (layer * FILL_SLOT.count(in_slot) + (FILL_SLOT[:n + 1].count(in_slot) + fills)) * 32)
                act.wait_ge(sem["pair_used"], value("pair_used", layer, reg + PAIR_BEFORE[p] + 1))
                act.activation(w_high[:, slot], raw[:, in_slot, (p % 2) * 1024:(p % 2) * 1024 + 1024], ACT.Copy
                               ).then_inc(sem["high_ready"], 1)

            def blocks_high(layer, stage, group, gain):
                tile = stage_tiles(stage)[0]
                blocks = group_blocks(stage, group)
                act.wait_ge(sem["blocks_turned"], value("blocks_turned", layer, 2 * stage + group + 1))
                for b in range(2):
                    source = bank[GROUP_BANKS[stage][b]]
                    if gain is None:
                        last = act.activation(tile[:, blocks[2 * b]:blocks[2 * b] + 2, :],
                                              source[:, :].rearrange("p (k s) -> p k s", k=2), ACT.Copy)
                    elif gain == G_SUBLN:
                        last = act.activation(tile[:, blocks[2 * b]:blocks[2 * b] + 2, :],
                                              source[:, :].rearrange("p (k s) -> p k s", k=2), ACT.Copy,
                                              scale=params[:, gain:gain + 1])
                    else:
                        for n in range(2):
                            kb = blocks[2 * b + n]
                            last = act.activation(tile[:, kb, :], source[:, n * S:(n + 1) * S], ACT.Copy,
                                                  scale=params[:, gain + kb:gain + kb + 1])
                    last.then_inc(sem["blocks_high"], 1)

            def norm_turned(layer, stage, gain, residuals, norm):
                blocks_high(layer, stage, 0, gain)
                act.wait_ge(sem["residual_done"], value("residual_done", layer, residuals))
                for half in range(HALVES):
                    last = act.activation(scratch[:, :, :].rearrange("p t c -> p (t c)"), x[:, half], ACT.Square,
                                          accum_out=norm_sq[:, half:half + 1])
                    if half == 0:
                        act.drain()
                last.then_inc(sem["squares_ready"], 1)
                blocks_high(layer, stage, 1, gain)
                act.wait_ge(sem["norm_ready"], value("norm_ready", layer, norm))

            def silu_gate(layer, chunk):
                act.wait_ge(sem["gate_up_done"], value("gate_up_done", layer, chunk))
                for half in range(HALVES):
                    act.activation(silu[:, half], bank[half][:, 0:FC], ACT.Silu, scale=norm_scale[:, half:half + 1]
                                   ).then_inc(sem["silu_ready"], 1)

            def hidden_high(layer, chunk):
                act.wait_ge(sem["hidden_turned"], value("hidden_turned", layer, chunk))
                act.activation(hT_high[:, :, :], bank[2][:, :].rearrange("p (k s) -> p k s", k=2), ACT.Copy
                               ).then_inc(sem["hidden_high"], 1)

            def ffn_chunks(layer, first, before):
                act.activation(sink_exp[:, 0:1], zero[:, 0:1].bitcast(F32), ACT.Silu)
                act.drain()
                with act.Fori(0, (CHUNKS - 1) // 2) as i:
                    for j in range(2):
                        p = first + 4 + 6 * j
                        for n in range(6):
                            if n == 3:
                                silu_gate(layer, i * 2 + (before + 1 + j))
                            if n == 5:
                                hidden_high(layer, i * 2 + (before + 1 + j))
                            high(layer, p + n, i * 12, i)

            def last_chunk(layer, first, before, following):
                p = first + FFN_PAIRS - 2
                high(layer, p)
                high(layer, p + 1)
                if following:
                    high(layer, p + 2)
                silu_gate(layer, before + CHUNKS)
                if following:
                    high(layer, p + 3)
                hidden_high(layer, before + CHUNKS)
                if following:
                    high(layer, p + 4)
                    high(layer, p + 5)

            def read_proj(layer, chunk):
                act.wait_ge(sem["proj_done"], value("proj_done", layer, chunk + 1))
                done = {3: 1, 4: 2, 5: 3}.get(chunk)
                if done:
                    act.wait_ge(sem["rope_done"], value("rope_done", layer, done))
                for half in range(HALVES):
                    source, scale = bank[2 * (chunk % 2) + half], norm_scale[:, half:half + 1]
                    if chunk >= 6:
                        c0 = 512 * (chunk - 6)
                        last = act.activation(gates[:, half, c0:c0 + 512], source[:, :],
                                              ACT.Copy if chunk in SIGMOID_AT else ACT.Sigmoid, scale=scale)
                        continue
                    parts = {0: [(qk_raw[0], 0, 0, 512)], 1: [(qk_raw[1], 0, 0, 512)], 2: [(values, 384, 0, 512)],
                             3: [(qk_raw[0], 0, 0, 512)], 4: [(values, 0, 0, 256), (qk_raw[1], 0, 256, 256)],
                             5: [(qk_raw[0], 0, 0, 128), (values, 256, 128, 128)]}[chunk]
                    for tile, to, c0, width in parts:
                        last = act.activation(tile[:, half, to:to + width], source[:, c0:c0 + width], ACT.Copy, scale=scale)
                last.then_inc(sem["proj_read"], 1)

            def head_squares(layer, chunk):
                buf, heads, _, _ = ROPE_HEADS[chunk]
                act.drain()
                if chunk:
                    act.wait_ge(sem["rope_done"], value("rope_done", layer, ROPE_CHUNKS[chunk] - 1))
                act.activation(scratch[:, :, 0:heads * DH], qk_raw[buf][:, :, 0:heads * DH], ACT.Square
                               ).then_inc(sem["head_squares"], 1)

            def copy_rope(layer, n):
                first, count, _ = ROPE_TURNS[n]
                act.wait_ge(sem["rope_turned"], value("rope_turned", layer, n + 1))
                for b in range(0, count, 2):
                    w = min(2, count - b)
                    last = act.activation(qk_blocks(first + b, w), bank[6 + b // 2][:, 0:w * S], ACT.Copy)
                last.then_inc(sem["rope_copied"], 1)

            def exps(layer, u):
                act.wait_ge(sem["scores_masked"], value("scores_masked", layer, u + 1))
                for t in range(2):
                    for half, cols in ((0, slice(0, P)), (1, slice(P, 3 * P))):
                        n = 2 * t + half
                        last = act.activation(probs[:, t, cols], probs[:, t, cols], ACT.Exp, bias=neg_max[:, n:n + 1],
                                              accum_out=row_sum[:, n:n + 1])
                if UNITS[u][0] == "B":
                    last = act.activation(sink_exp[:, :], sink_diff[:, :], ACT.Exp)
                last.then_inc(sem["exps_ready"], 1)

            def copy_probs(layer, u):
                act.wait_ge(sem["probs_turned"], value("probs_turned", layer, u + 1))
                for t in range(1 if UNITS[u][0] == "C" else 2):
                    last = act.activation(probsT[:, t], bank[6 + t][:, 0:3 * P], ACT.Copy)
                last.then_inc(sem["probs_copied"], 1)

            def read_context(layer, u):
                act.wait_ge(sem["context_done"], value("context_done", layer, u + 1))
                if UNITS[u][0] == "C":
                    c0 = context_column(u, 0)
                    last = act.activation(o_nat[:, :, c0:c0 + P], bank[7][:, 0:S].rearrange("p (t c) -> p t c", t=2), ACT.Copy)
                else:
                    for t in range(2):
                        c0 = context_column(u, t)
                        for half in range(HALVES):
                            last = act.activation(o_nat[:, half, c0:c0 + DH], bank[6 + t][:, 384 + half * DH:384 + half * DH + DH],
                                                  ACT.Copy, scale=inv_sum[:, 2 * t + half:2 * t + half + 1])
                last.then_inc(sem["context_read"], 1)

            def mixing(layer):
                norm_turned(layer, ST_MIX, G_MIX, 4, 2)
                for m in range(4, FFN2_0 - MIX0 + 4):
                    for chunk, end in enumerate(PROJ_END):
                        if m == end + RING:
                            read_proj(layer, chunk)
                    for chunk, at in SQUARES_AT.items():
                        if m == at:
                            head_squares(layer, chunk)
                    for n, (_, _, pos) in enumerate(ROPE_TURNS):
                        if m == pos + RING - 1:
                            copy_rope(layer, n)
                    for u, (_, _, _, pos) in enumerate(UNITS):
                        if m == pos + 3 + RING - 1:
                            copy_probs(layer, u)
                        if m == pos + 4 + RING - 1:
                            read_context(layer, u)
                    for u, (_, _, _, pos) in enumerate(UNITS):
                        if m == pos + RING:
                            exps(layer, u)
                    if m == SUBLN_AT:
                        act.drain()
                        act.wait_ge(sem["rope_done"], value("rope_done", layer, 5))
                        act.activation(scratch[:, :, :], o_nat[:, :, 512:1024], ACT.Square).then_inc(sem["subln_squares"], 1)
                    for group, pos in enumerate(O_TURNS):
                        if m == pos + RING - 1:
                            blocks_high(layer, ST_O, group, None if group else G_SUBLN)
                    for chunk, at in SIGMOID_AT.items():
                        if m == at:
                            v = gates[:, :, 512 * (chunk - 6):512 * (chunk - 5)]
                            act.drain()
                            act.activation(v, v, ACT.Sigmoid)
                    if m == MERGE_B_AT:
                        blocks_high(layer, ST_MERGED, 0, None)
                        blocks_high(layer, ST_MERGED, 1, None)
                    high(layer, MIX0 + m)

            for n, name in enumerate(("ffn1_norm", "mix_norm", "ffn2_norm")):
                act.dma_start(gain_rows[16 * n:16 * n + 16, :], a[name].rearrange("l (k p) -> (l k) p", p=P)).then_inc(rows_loaded, 16)
            act.dma_start(gain_rows[48:50, :], a["diff_subln"]).then_inc(rows_loaded, 16)
            act.dma_start(trig[:, :, :, :], a["trig"]).then_inc(params_loaded, 16)
            for i, name in enumerate(("diff_q_norm", "diff_k_norm", "moba_q_norm", "moba_k_norm", "swa_q_norm", "swa_k_norm")):
                act.dma_start(params_all[:, :, ROPE_GAIN + DH * i:ROPE_GAIN + DH * (i + 1)],
                              a[name].unsqueeze(0).to_broadcast([P, DEPTH, DH])).then_inc(params_loaded, 16)
            act.dma_start(params_all[:, :, SINK:SINK + 4], a["swa_sinks"].unsqueeze(0).to_broadcast([P, DEPTH, 4])
                          ).then_inc(params_loaded, 16)
            for i, name in enumerate(("diff_lambda_q1", "diff_lambda_k1", "diff_lambda_q2", "diff_lambda_k2")):
                act.dma_start(lam_vec[:, i], a[name].unsqueeze(0).to_broadcast([P, DEPTH, DH])).then_inc(params_loaded, 16)
            act.wait_ge(lambda_sums, 1)
            act.activation(small[:, 1, 0:2 * DEPTH], small[:, 0, 0:2 * DEPTH], ACT.Exp).then_inc(lambda_exps, 1)
            act.wait_ge(constants_ready, 1)
            with act.Fori(0, DEPTH) as layer:
                for p in range(4):
                    high(layer, p)
                act.wait_ge(sem["params_ready"], value("params_ready", layer, 1))
                norm_turned(layer, ST_FFN1, G_FFN1, 0, 1)
                ffn_chunks(layer, 0, 0)
                last_chunk(layer, 0, 0, True)
                mixing(layer)
                norm_turned(layer, ST_FFN2, G_FFN2, 8, 3)
                ffn_chunks(layer, FFN2_0, CHUNKS)
                last_chunk(layer, FFN2_0, CHUNKS, False)

        @block.vector
        def _(dve):
            def low(layer, p, p_reg=None):
                slot = PAIR_SLOT[p]
                reg = 0 if p_reg is None else p_reg
                dve.wait_ge(sem["high_ready"], value("high_ready", layer, reg + p + 1))
                dve.tensor_tensor(w_low[:, slot], raw[:, FILL_SLOT[p // 2], (p % 2) * 1024:(p % 2) * 1024 + 1024],
                                  w_high[:, slot].bitcast(F32), ALU.subtract).then_inc(sem["low_ready"], 1)

            def blocks_low(layer, stage, group, gain):
                high_tile, low_tile = stage_tiles(stage)
                blocks = group_blocks(stage, group)
                for b in range(2):
                    source = bank[GROUP_BANKS[stage][b]]
                    dve.wait_ge(sem["blocks_high"], value("blocks_high", layer, 4 * stage + 2 * group + b + 1))
                    if gain is None or gain == G_SUBLN:
                        kb = blocks[2 * b]
                        last = dve.scalar_tensor_tensor(
                            low_tile[:, kb:kb + 2, :], source[:, :].rearrange("p (k s) -> p k s", k=2),
                            1.0 if gain is None else params[:, gain:gain + 1], high_tile[:, kb:kb + 2, :].bitcast(F32),
                            ALU.mult, ALU.subtract)
                    else:
                        for n in range(2):
                            kb = blocks[2 * b + n]
                            last = dve.scalar_tensor_tensor(
                                low_tile[:, kb, :], source[:, n * S:(n + 1) * S], params[:, gain + kb:gain + kb + 1],
                                high_tile[:, kb, :].bitcast(F32), ALU.mult, ALU.subtract)
                    last.then_inc(sem["blocks_low"], 1)

            def residual(layer, n, product, factor):
                half, cols = QUARTERS[n]
                dve.wait_ge(sem["product_done"], value("product_done", layer, product + n + 1))
                v = x[:, half, 512 * cols:512 * cols + 512]
                dve.scalar_tensor_tensor(v, quarter(half, cols)[:, :], factor, v, ALU.mult, ALU.add
                                         ).then_inc(sem["residual_done"], 1)

            def inverse_root(out, total, n, shape, count):
                v, guess, a0, b0 = (small[:, k, 0:n] for k in (2, 3, 4, 5))
                dve.tensor_scalar(v, total, 1.0 / count, EPS, ALU.mult, ALU.add)
                dve.drain()
                dve.tensor_scalar(a0.bitcast(I32), v.bitcast(I32), 1, None, ALU.logical_shift_right)
                dve.drain()
                dve.tensor_scalar(guess.bitcast(I32), a0.bitcast(I32), -1.0, float(0x5F3759DF), ALU.mult, ALU.add)
                dve.drain()
                for step in range(3):
                    dve.tensor_tensor(a0, guess, guess, ALU.mult)
                    dve.drain()
                    dve.scalar_tensor_tensor(b0, a0, -0.5, v, ALU.mult, ALU.mult)
                    dve.drain()
                    if step < 2:
                        dve.scalar_tensor_tensor(guess, b0, 1.5, guess, ALU.add, ALU.mult)
                        dve.drain()
                return dve.scalar_tensor_tensor(out, shape(b0), 1.5, shape(guess), ALU.add, ALU.mult)

            def norm(layer, n):
                dve.wait_ge(sem["squares_ready"], value("squares_ready", layer, n))
                inverse_root(norm_scale[:, :], norm_sq[:, :], HALVES, lambda v: v, D).then_inc(sem["norm_ready"], 1)

            def multiply_hidden(layer, chunk):
                for half in range(HALVES):
                    dve.wait_ge(sem["silu_ready"], value("silu_ready", layer, 2 * chunk + (half - 1)))
                    last = dve.scalar_tensor_tensor(hidden[:, half], bank[half][:, FC:2 * FC], norm_scale[:, half:half + 1],
                                                    silu[:, half], ALU.mult, ALU.mult)
                last.then_inc(sem["hidden_ready"], 1)

            def hidden_low(layer, chunk):
                dve.wait_ge(sem["hidden_high"], value("hidden_high", layer, chunk))
                dve.tensor_tensor(hT_low[:, :, :], bank[2][:, :].rearrange("p (k s) -> p k s", k=2),
                                  hT_high[:, :, :].bitcast(F32), ALU.subtract).then_inc(sem["hidden_low"], 1)

            def ffn_chunks(layer, first, before):
                with dve.Fori(0, (CHUNKS - 1) // 2) as i:
                    for j in range(2):
                        p = first + 4 + 6 * j
                        for n in range(6):
                            if n == 3:
                                multiply_hidden(layer, i * 2 + (before + 1 + j))
                            if n == 5:
                                hidden_low(layer, i * 2 + (before + 1 + j))
                            low(layer, p + n, i * 12)

            def last_chunk(layer, first, before, following):
                p = first + FFN_PAIRS - 2
                low(layer, p)
                low(layer, p + 1)
                if following:
                    low(layer, p + 2)
                multiply_hidden(layer, before + CHUNKS)
                if following:
                    low(layer, p + 3)
                hidden_low(layer, before + CHUNKS)
                if following:
                    low(layer, p + 4)
                    low(layer, p + 5)

            def add_and_turn(layer, stage, gain, product, factor, n):
                for q in range(3):
                    residual(layer, q, product, factor)
                blocks_low(layer, stage, 0, gain)
                residual(layer, 3, product, factor)
                blocks_low(layer, stage, 1, gain)
                norm(layer, n)

            def rope_tables(layer):
                g = params[:, ROPE_GAIN:PARAMS].rearrange("p (i d) -> p i d", i=6)
                shape = [P, 6, HALVES, DH]
                dve.tensor_tensor(rope_cos[:, :, :, :], g.unsqueeze(2).to_broadcast(shape),
                                  trig[:, 0].unsqueeze(1).to_broadcast(shape), ALU.mult)
                h = DH // 2
                for to, of in ((slice(0, h), slice(h, DH)), (slice(h, DH), slice(0, h))):
                    dve.tensor_tensor(rope_sin[:, :, :, to], g[:, :, of].unsqueeze(2).to_broadcast([P, 6, HALVES, h]),
                                      trig[:, 1, :, to].unsqueeze(1).to_broadcast([P, 6, HALVES, h]), ALU.mult)
                dve.drain()

            def rope(layer, chunk):
                buf, heads, scale0, parts = ROPE_HEADS[chunk]
                scales = head_scale[:, :, scale0:scale0 + heads]
                total = small[:, 6, 0:HALVES * heads]
                dve.wait_ge(sem["head_squares"], value("head_squares", layer, ROPE_CHUNKS[chunk]))
                dve.tensor_reduce(total.rearrange("p (t h) -> p t h", t=HALVES),
                                  scratch[:, :, 0:heads * DH].rearrange("p t (h d) -> p t h d", d=DH), axis=AXIS_X, op=ALU.add)
                dve.drain()
                inverse_root(scales, total, HALVES * heads, lambda v: v.rearrange("p (t h) -> p t h", t=HALVES), DH)
                dve.drain()
                h = DH // 2
                c0 = 0
                for table, count, is_q in parts:
                    v = qk_raw[buf][:, :, c0 * DH:(c0 + count) * DH].rearrange("p t (h d) -> p t h d", d=DH)
                    w = scratch[:, :, c0 * DH:(c0 + count) * DH].rearrange("p t (h d) -> p t h d", d=DH)
                    r = scales[:, :, c0:c0 + count]
                    if is_q:
                        dve.tensor_scalar(r, r, SCALE, None, ALU.mult)
                    else:
                        dve.tensor_tensor(v, v, r.unsqueeze(3).to_broadcast([P, HALVES, count, DH]), ALU.mult)
                        dve.drain()
                    for to, of in ((slice(0, h), slice(h, DH)), (slice(h, DH), slice(0, h))):
                        dve.tensor_tensor(w[:, :, :, to], v[:, :, :, of],
                                          rope_sin[:, table, :, to].unsqueeze(2).to_broadcast([P, HALVES, count, h]), ALU.mult)
                    dve.drain()
                    dve.tensor_tensor(v, v, rope_cos[:, table].unsqueeze(2).to_broadcast([P, HALVES, count, DH]), ALU.mult)
                    c0 += count
                dve.drain()
                before = {1: 1, 3: 2, 4: 3}.get(chunk)
                if before:
                    dve.wait_ge(sem["rope_turned"], value("rope_turned", layer, before))
                if chunk == 4:
                    for half in range(HALVES):
                        out = roped[:, half, P:P + 4 * DH].rearrange("p (b a d) -> p a b d", b=2, a=2)
                        v, w = (t[:, half, 0:4 * DH].rearrange("p (a b d) -> p a b d", a=2, b=2) for t in (qk_raw[buf], scratch))
                        last = dve.tensor_tensor(out, v, w, ALU.add)
                else:
                    out0 = P + 4 * DH if chunk == 5 else 0
                    last = dve.tensor_tensor(roped[:, :, out0:out0 + heads * DH], qk_raw[buf][:, :, 0:heads * DH],
                                             scratch[:, :, 0:heads * DH], ALU.add)
                last.then_inc(sem["rope_done"], 1)

            def mask_scores(layer, u):
                kind = UNITS[u][0]
                dve.wait_ge(sem["scores_done"], value("scores_done", layer, u + 1))
                if u > 0:
                    dve.wait_ge(sem["probs_turned"], value("probs_turned", layer, u))
                dve.sem_inc(units_started, 1)
                for t in range(2):
                    for half, cols in ((0, slice(0, P)), (1, slice(P, 3 * P))):
                        mask = masks[:, 1] if half == 0 else masks[:, 2:4] if kind == "B" else masks[:, 0:2]
                        out, source = probs[:, t, cols], bank[4 + t][:, cols]
                        if half:
                            out, source = (v.rearrange("p (b k) -> p b k", b=2) for v in (out, source))
                        dve.tensor_tensor_reduce(out=out, in0=source, in1=mask, scale=query_scale(u, t, half), scalar=-3e38,
                                                 op0=ALU.add, op1=ALU.max, accum_out=row_max[:, 2 * t + half:2 * t + half + 1])
                dve.drain()
                if kind == "B":
                    for t in range(2):
                        n = SINK + (u - 6) + 2 * t
                        v = row_max[:, 2 * t:2 * t + 2]
                        dve.tensor_scalar(v, v, params[:, n:n + 1], None, ALU.max)
                    dve.drain()
                    for t in range(2):
                        n = SINK + (u - 6) + 2 * t
                        dve.tensor_scalar(sink_diff[:, 2 * t:2 * t + 2], row_max[:, 2 * t:2 * t + 2], params[:, n:n + 1], -1.0,
                                          ALU.subtract, ALU.mult)
                dve.tensor_scalar(neg_max[:, :], row_max[:, :], -1.0, None, ALU.mult).then_inc(sem["scores_masked"], 1)

            def normalise(layer, u):
                kind = UNITS[u][0]
                dve.wait_ge(sem["exps_ready"], value("exps_ready", layer, u + 1))
                if kind == "B":
                    dve.tensor_tensor(row_sum[:, :], row_sum[:, :], sink_exp[:, :], ALU.add)
                    dve.drain()
                last = dve.reciprocal(inv_sum[:, :], row_sum[:, :])
                if kind == "C":
                    dve.drain()
                    dve.tensor_scalar(inv_sum[:, 2:4], inv_sum[:, 2:4], params[:, NEG_LAM:NEG_LAM + 1], None, ALU.mult)
                    dve.drain()
                    for half, cols in ((0, slice(0, P)), (1, slice(P, 3 * P))):
                        dve.tensor_scalar(probs[:, 1, cols], probs[:, 1, cols], inv_sum[:, 2 + half:3 + half], None, ALU.mult)
                    dve.drain()
                    for half, cols in ((0, slice(0, P)), (1, slice(P, 3 * P))):
                        last = dve.scalar_tensor_tensor(probs[:, 0, cols], probs[:, 0, cols], inv_sum[:, half:half + 1],
                                                        probs[:, 1, cols], ALU.mult, ALU.add)
                last.then_inc(sem["probs_ready"], 1)

            def subln(layer):
                dve.wait_ge(sem["subln_squares"], value("subln_squares", layer, 1))
                total = small[:, 6, 0:HALVES * 4]
                dve.tensor_reduce(total.rearrange("p (t h) -> p t h", t=HALVES),
                                  scratch[:, :, :].rearrange("p t (h d) -> p t h d", d=P), axis=AXIS_X, op=ALU.add)
                dve.drain()
                scales = small[:, 7, 0:HALVES * 4]
                inverse_root(scales, total, HALVES * 4, lambda v: v, P)
                dve.drain()
                v = o_nat[:, :, 512:1024].rearrange("p t (h d) -> p t h d", d=P)
                r = scales.rearrange("p (t h) -> p t h", t=HALVES).unsqueeze(3).to_broadcast([P, HALVES, 4, P])
                dve.tensor_tensor(v, v, r, ALU.mult).then_inc(sem["subln_ready"], 1)

            def gate(branch, n):
                half, cols = QUARTERS[n]
                c0 = branch * D + 512 * cols
                return gates[:, half, c0:c0 + 512]

            def merged_quarter(n):
                half, cols = QUARTERS[n]
                return merged[:, half, 512 * cols:512 * cols + 512]

            def merge_c(layer):
                dve.wait_ge(sem["product_done"], value("product_done", layer, 5))
                dve.wait_ge(sem["proj_read"], value("proj_read", layer, len(PROJ)))
                for n in range(4):
                    dve.tensor_tensor(merged_quarter(n), quarter(*QUARTERS[n])[:, :], gate(2, n), ALU.mult
                                      ).then_inc(sem["merged"], 1)

            def merge(layer, source, branch, n, product):
                t = scratch[:, n % 2]
                dve.drain()
                dve.wait_ge(sem["product_done"], value("product_done", layer, product))
                dve.tensor_tensor(t, source[:, :], gate(branch, n), ALU.mult)
                dve.drain()
                dve.tensor_tensor(merged_quarter(n), merged_quarter(n), t, ALU.add).then_inc(sem["merged"], 1)

            def mixing(layer):
                add_and_turn(layer, ST_MIX, G_MIX, 0, 0.5, 2)
                for m in range(4, FFN2_0 - MIX0 + 4):
                    for u, (_, _, _, pos) in enumerate(UNITS):
                        if m == pos + 7:
                            normalise(layer, u)
                    for u, (_, _, _, pos) in enumerate(UNITS):
                        if m == pos + 5:
                            mask_scores(layer, u)
                    for chunk, at in ROPE_AT.items():
                        if m == at:
                            rope(layer, chunk)
                    if m == SUBLN_AT + 1:
                        subln(layer)
                    for group, pos in enumerate(O_TURNS):
                        if m == pos + RING:
                            blocks_low(layer, ST_O, group, None if group else G_SUBLN)
                    if m == MERGE_C_AT:
                        merge_c(layer)
                    if m == MERGE_A_AT:
                        for n, (half, cols) in enumerate(QUARTERS):
                            merge(layer, bank[half + 2 * cols], 0, n, 6)
                    if m == MERGE_B_AT:
                        for n, (half, cols) in enumerate(QUARTERS):
                            if n == 3:
                                blocks_low(layer, ST_MERGED, 0, None)
                            merge(layer, quarter(half, cols), 1, n, 7 + n)
                        blocks_low(layer, ST_MERGED, 1, None)
                    low(layer, MIX0 + m)

            dve.sem_inc(sem["low_ready"], CREDIT["low_ready"])
            dve.wait_ge(x_loaded, 32)
            dve.sem_inc(sem["residual_done"], CREDIT["residual_done"])
            dve.wait_ge(constants_ready, 1)
            dve.wait_ge(gains_turned, 1)
            for i, g in enumerate((G_FFN1, G_MIX, G_FFN2)):
                dve.tensor_copy(params_all[:, :, g:g + KB], bank[0][:, 16 * i:16 * i + 16].rearrange("p (l k) -> p l k", l=DEPTH))
            for l in range(DEPTH):
                dve.tensor_scalar(params_all[:, l, G_SUBLN:G_SUBLN + 1], bank[0][:, 48 + l:49 + l], 1.0 - LAM_INIT[l], None, ALU.mult)
            dve.wait_ge(params_loaded, 16 * 12)
            for l in range(DEPTH):
                for i in range(2):
                    n = 2 * l + i
                    dve.tensor_tensor_reduce(out=probsT[:, 1, n * DH:(n + 1) * DH], in0=lam_vec[:, 2 * i, l], in1=lam_vec[:, 2 * i + 1, l],
                                             scale=1.0, scalar=0.0, op0=ALU.mult, op1=ALU.add,
                                             accum_out=small[:, 0, n:n + 1])
            dve.drain().then_inc(lambda_sums, 1)
            dve.wait_ge(lambda_exps, 1)
            for l in range(DEPTH):
                dve.tensor_scalar(small[:, 7, l:l + 1], small[:, 1, 2 * l + 1:2 * l + 2], -LAM_INIT[l], None, ALU.add)
            dve.drain()
            for l in range(DEPTH):
                dve.tensor_tensor(params_all[:, l, NEG_LAM:NEG_LAM + 1], small[:, 7, l:l + 1], small[:, 1, 2 * l:2 * l + 1], ALU.subtract)
            dve.drain()
            with dve.Fori(0, DEPTH) as layer:
                dve.tensor_copy(params[:, :], params_all[:, bass.ds(layer, 1), :].rearrange("p o c -> p (o c)")
                                ).then_inc(sem["params_ready"], 1)
                for p in range(4):
                    low(layer, p)
                dve.drain()
                blocks_low(layer, ST_FFN1, 0, G_FFN1)
                blocks_low(layer, ST_FFN1, 1, G_FFN1)
                norm(layer, 1)
                rope_tables(layer)
                ffn_chunks(layer, 0, 0)
                last_chunk(layer, 0, 0, True)
                mixing(layer)
                add_and_turn(layer, ST_FFN2, G_FFN2, 10, 1.0, 3)
                ffn_chunks(layer, FFN2_0, CHUNKS)
                last_chunk(layer, FFN2_0, CHUNKS, False)
                for q in range(4):
                    residual(layer, q, 14, 0.5)


_INS = ["x", "ffn1_norm", "ffn1_w_gate", "ffn1_w_up", "ffn1_w_down", "mix_norm", "w_in", "moba_q_norm", "moba_k_norm",
        "swa_q_norm", "swa_k_norm", "swa_sinks", "diff_q_norm", "diff_k_norm", "diff_lambda_q1", "diff_lambda_k1",
        "diff_lambda_q2", "diff_lambda_k2", "diff_subln", "w_branch_a", "w_branch_b", "w_branch_c", "w_out", "ffn2_norm",
        "ffn2_w_gate", "ffn2_w_up", "ffn2_w_down"]


def rotary_constants():
    inv_freq = np.float32(10000.0) ** (-np.arange(0, DH, 2, dtype=np.float32) / np.float32(DH))
    angle = np.arange(S, dtype=np.float32)[:, None] * inv_freq[None, :]
    cos, sin = np.cos(angle), np.sin(angle)
    table = np.stack([np.concatenate([cos, cos], 1), np.concatenate([-sin, sin], 1)])
    return np.ascontiguousarray(table.reshape(2, HALVES, P, DH).transpose(2, 0, 1, 3).astype(np.float32))


def kernel(**inputs):
    import concourse.bacc as bacc
    from concourse.bass_utils import run_bass_kernel_spmd

    nc = bacc.Bacc("TRN2", target_bir_lowering=False, num_devices=1)
    arrays = {name: np.ascontiguousarray(inputs[name]) for name in _INS}
    arrays["trig"] = rotary_constants()
    tensors = {name: nc.dram_tensor(f"in_{name}", v.shape, mybir.dt.from_np(v.dtype), kind="ExternalInput").ap()
               for name, v in arrays.items()}
    tensors["out"] = nc.dram_tensor("out", (1, S, D), F32, kind="ExternalOutput").ap()
    build(nc, tensors)
    r = run_bass_kernel_spmd(nc, [{f"in_{name}": v for name, v in arrays.items()}], core_ids=[0])
    return r.results[0]["out"]
```

```python
from contextlib import ExitStack

import numpy as np

import concourse.bass as bass
from concourse import mybir

F32 = mybir.dt.float32
F32R = mybir.dt.float32r
I32 = mybir.dt.int32
ALU = mybir.AluOpType
ACT = mybir.ActivationFunctionType
AXIS_X = mybir.AxisListType.X

P = 128
S = 256
HALVES = S // P
D = 1024
KB = D // P
F = 2816
FC = 256
CHUNKS = F // FC
DH = 64
DEPTH = 2
EPS = 1e-6
NEG = -1e30
SCALE = DH ** -0.5
LAM_INIT = [0.8 - 0.6 * float(np.exp(-0.3 * layer)) for layer in range(DEPTH)]

QA, KA, VA, QB, KBC, VB, QC, KC, VC, GATES = 0, 256, 512, 768, 1024, 1152, 1280, 1792, 2304, 2816
PROJ = [(QC, 512), (KC, 512), (VC, 512), (QA, 512), (VA, 512), (KBC, 256)] + [(GATES + 512 * g, 512) for g in range(6)]

RING = 6
FFN_PAIRS = CHUNKS * 6
PROJ_PAIRS = sum(width // 128 for _, width in PROJ)
BRANCH_PAIRS = KB
OUT_PAIRS = KB
MIX0 = FFN_PAIRS
BRANCH0 = MIX0 + PROJ_PAIRS
OUT0 = BRANCH0 + BRANCH_PAIRS
FFN2_0 = OUT0 + OUT_PAIRS
PAIRS = FFN2_0 + FFN_PAIRS
FILLS = PAIRS // 2

G_FFN1, G_MIX, G_FFN2, G_SUBLN = 0, 8, 16, 24
LAM_INIT_AT = 25
GAINS = 26
ROPE_GAIN, LAM_VEC, SINK = 0, 6 * DH, 10 * DH
PARAMS = SINK + 4
GAIN_ROWS = (3 * KB + 1) * DEPTH
ST_FFN1, ST_MIX, ST_O, ST_MERGED, ST_FFN2 = range(5)

UNITS = [("C", h, 4 + h, 16 + 3 * h) for h in range(4)] + [("A", 8 + j, 10 + j, 28 + 3 * j) for j in range(2)] \
    + [("B", 12 + j, 14, 34 + 3 * j) for j in range(2)]
ROPE_TURNS = [(0, 4, 10), (4, 4, 15), (8, 4, 25), (12, 3, 31)]
O_TURNS = [37, 44]
SILU_AT, HIDDEN_TURN = 4, 2
TURN_AFTER, CONTEXT_AFTER = 4, 5

PER_LAYER = {
    "pair_used": PAIRS, "high_ready": PAIRS, "low_ready": PAIRS,
    "blocks_turned": 10, "blocks_high": 20, "blocks_low": 20,
    "gate_up_done": 2 * CHUNKS, "silu_ready": 2 * CHUNKS * HALVES, "hidden_ready": 2 * CHUNKS,
    "hidden_turned": 4 * CHUNKS, "hidden_high": 4 * CHUNKS, "hidden_low": 4 * CHUNKS,
    "product_done": 24, "residual_done": 12, "merged": 8, "a_gated": 4, "a_added": 4,
    "squares_ready": 3, "norm_guessed": 3, "norm_ready": 3, "gains_copied": 1,
    "proj_done": len(PROJ), "proj_read": len(PROJ), "head_squares": 5, "heads_scaled": 5, "tables_ready": 1, "rope_done": 7,
    "rope_turned": 4, "rope_copied": 4,
    "scores_done": 8, "scores_masked": 8, "exps_ready": 8, "probs_ready": 8, "probs_turned": 8,
    "probs_copied": 8, "context_done": 8, "context_read": 8, "subln_squares": 1, "subln_ready": 1,
    "lambda_sums": 1, "lambda_exps": 1,
}
CREDIT = {"pair_used": RING, "low_ready": 2 * RING, "product_done": 4, "residual_done": 4}


def ring_slots(items, mix_first, mix_items):
    full_rounds = next(a for a in range(mix_items // RING, -1, -1)
                       if (mix_items - RING * a) % (RING - 1) == 0)
    short_rounds = (mix_items - RING * full_rounds) // (RING - 1)
    slots = [n % RING for n in range(mix_first)]
    first = mix_first % RING
    order = [(first + k) % RING for k in range(RING)]
    slots += order[:-1] * short_rounds + order * full_rounds
    slots += [(first + k) % RING for k in range(items - len(slots))]
    assert slots[-1] == RING - 1
    return slots


def earlier(slots):
    return [max(m for m in range(n - len(slots), n) if slots[m] == slots[n]) for n in range(len(slots))]


FILL_SLOT = ring_slots(FILLS, MIX0 // 2, (FFN2_0 - MIX0) // 2)
PAIR_SLOT = ring_slots(PAIRS, MIX0, FFN2_0 - MIX0)
FILL_BEFORE, PAIR_BEFORE = earlier(FILL_SLOT), earlier(PAIR_SLOT)


def build(nc, a):
    ctx = ExitStack()
    with ctx:
        def sb(name, shape, dt=F32):
            return ctx.enter_context(nc.sbuf_tensor(name, shape, dt))

        raw = sb("raw", [P, RING, 2048])
        w_high = sb("w_high", [P, RING, 1024], F32R)
        w_low = sb("w_low", [P, RING, 1024], F32R)
        x = sb("x", [P, HALVES, D])
        xT_high = sb("xT_high", [P, KB, S], F32R)
        xT_low = sb("xT_low", [P, KB, S], F32R)
        oT_high = sb("oT_high", [P, KB, S], F32R)
        oT_low = sb("oT_low", [P, KB, S], F32R)
        gates = sb("gates", [P, HALVES, 3 * D])
        values = sb("values", [P, HALVES, 896])
        o_nat = sb("o_nat", [P, HALVES, D])
        work = sb("work", [P, 2048])
        silu = work[:, 0:512].rearrange("p (t f) -> p t f", t=HALVES)
        hidden = work[:, 512:1024].rearrange("p (t f) -> p t f", t=HALVES)
        hT_high = sb("hT_high", [P, 2, S], F32R)
        hT_low = sb("hT_low", [P, 2, S], F32R)
        qk_raw = [work[:, 1024 * b:1024 * b + 1024].rearrange("p (t c) -> p t c", t=HALVES) for b in range(2)]
        merged = work[:, :].rearrange("p (t c) -> p t c", t=HALVES)
        roped = o_nat[:, :, 0:512]
        scratch = sb("scratch", [P, HALVES, 512])
        probs_of = [sb(f"probs{n}", [P, 2, 384]) for n in range(2)]
        probsT = sb("probsT", [P, 2, 384])
        ident = sb("ident", [P, P])
        masks = sb("masks", [P, 4, P])
        zero = sb("zero", [P, P], F32R)
        trig = sb("trig", [P, 2, HALVES, DH])
        gains_all = sb("gains_all", [P, DEPTH, GAINS])
        gains = sb("gains", [P, GAINS])
        params = sb("params", [P, PARAMS])
        rope_cos, rope_sin = (gates[:, n, 4 * 512:4 * 512 + 12 * DH].rearrange("p (i t d) -> p i t d", i=6, t=HALVES) for n in range(2))
        gain_rows = probsT[:, 0, 0:P]
        small = sb("small", [P, 8, 16])
        head_scale = sb("head_scale", [P, HALVES, 30])
        norm_sq, norm_scale, neg_lam = (small[:, 1, n:n + 2] for n in (4, 6, 8))
        stats = sb("stats", [P, 6, 2, 4])
        row_max_of, neg_max_of, row_sum_of, inv_sum_of, sink_diff_of, sink_exp_of = (
            [stats[:, i, n] for n in range(2)] for i in range(6))
        bank = [ctx.enter_context(nc.psum_tensor(f"bank{b}", [P, 512], F32)) for b in range(8)]

        sem = {name: ctx.enter_context(nc.semaphore(name)) for name in PER_LAYER}
        fill_landed = [ctx.enter_context(nc.semaphore(f"fill_landed{n}")) for n in range(RING)]
        x_loaded = ctx.enter_context(nc.semaphore("x_loaded"))
        rows_loaded = ctx.enter_context(nc.semaphore("rows_loaded"))
        trig_loaded = ctx.enter_context(nc.semaphore("trig_loaded"))
        params_loaded = ctx.enter_context(nc.semaphore("params_loaded"))
        constants_ready = ctx.enter_context(nc.semaphore("constants_ready"))
        gains_turned = ctx.enter_context(nc.semaphore("gains_turned"))
        gains_ready = ctx.enter_context(nc.semaphore("gains_ready"))
        lam_init_ready = ctx.enter_context(nc.semaphore("lam_init_ready"))
        sp_waited = ctx.enter_context(nc.semaphore("sp_waited"))
        dve_waited = ctx.enter_context(nc.semaphore("dve_waited"))
        stored = ctx.enter_context(nc.semaphore("stored"))
        block = ctx.enter_context(nc.Block())

        def qk_blocks(first, count):
            base, per_half, c0 = (0, 4, 0) if first < 8 else (8, 2, 1024) if first < 12 else (12, 2, 1536)
            half, n = divmod(first - base, per_half)
            return gates[:, half, c0 + n * S:c0 + (n + count) * S]

        GROUP_BANKS = {ST_FFN1: (2, 3), ST_MIX: (2, 3), ST_O: (6, 7), ST_MERGED: (2, 3), ST_FFN2: (2, 3)}

        def hidden_blocks(banks):
            return [bank[banks[fb]][:, (fb if banks[0] == banks[1] else 0) * S:][:, 0:S] for fb in range(2)]

        QUARTERS = [(0, 0), (1, 0), (0, 1), (1, 1)]

        def quarter(half, cols):
            return bank[4 + half + 2 * cols]

        def gate(branch, n):
            half, cols = QUARTERS[n]
            c0 = branch * D + 512 * cols
            return gates[:, half, c0:c0 + 512]

        def gated(n):
            half, cols = QUARTERS[n]
            return o_nat[:, half, 512 * cols:512 * cols + 512]

        def merged_quarter(n):
            half, cols = QUARTERS[n]
            return merged[:, half, 512 * cols:512 * cols + 512]

        def a_quarter(half, cols):
            return bank[half + 2 * cols]

        def group_blocks(stage, group):
            first = 4 * (1 - group) if stage == ST_O else 4 * group
            return range(first, first + 4)

        def stage_tiles(stage):
            return (oT_high, oT_low) if stage == ST_O else (xT_high, xT_low)

        def banks_split(stage, group, n):
            return 4 * stage + 2 * group + n + 1

        def value(name, layer, k):
            return layer * PER_LAYER[name] + (k + CREDIT.get(name, 0))

        @block.sync
        def _(sp):
            def fill(layer, n, sources, n_reg=None):
                slot = FILL_SLOT[n]
                sp.wait_ge(sem["low_ready"], value("low_ready", layer, (0 if n_reg is None else n_reg) + 2 * FILL_BEFORE[n] + 2))
                sp.sem_inc(sp_waited, 1)
                for dst, src in sources(raw[:, slot]):
                    sp.dma_start(dst, src).then_inc(fill_landed[slot], 16)

            def rows(w, layer, k0, nk, c0, width):
                return w[bass.ds(layer, 1), k0 * P:(k0 + nk) * P, c0:c0 + width].rearrange("o (k p) c -> p (o k) c", p=P)

            def gate_up(wg, wu, layer, c, k0):
                def sources(slot):
                    v = slot.rearrange("p (k g c) -> p k g c", k=4, g=2)
                    for g, w in enumerate((wg, wu)):
                        yield v[:, :, g], w[bass.ds(layer, 1), k0 * P:(k0 + 4) * P, bass.ds(c * FC, FC)].rearrange(
                            "o (k p) c -> p (o k) c", p=P)
                return sources

            def down(wd, layer, c):
                def sources(slot):
                    v = slot.rearrange("p (k c) -> p k c", k=2)
                    for k in range(2):
                        yield v[:, k], wd[bass.ds(layer, 1), bass.ds(c * FC + k * P, P), :].rearrange("o p c -> p (o c)")
                return sources

            def wide(w, layer, k0):
                def sources(slot):
                    v = slot.rearrange("p (k c) -> p k c", k=2)
                    for k in range(2):
                        yield v[:, k], w[bass.ds(layer, 1), (k0 + k) * P:(k0 + k + 1) * P, :].rearrange("o p c -> p (o c)")
                return sources

            def proj(layer, c0, width, k0, nk):
                def sources(slot):
                    v = slot.rearrange("p (k c) -> p k c", k=nk)
                    for h in range(2):
                        yield v[:, h * nk // 2:(h + 1) * nk // 2], rows(a["w_in"], layer, k0 + h * nk // 2, nk // 2, c0, width)
                return sources

            def ffn(layer, first, wg, wu, wd):
                n = first // 2
                fill(layer, n, gate_up(wg, wu, layer, 0, 0))
                fill(layer, n + 1, gate_up(wg, wu, layer, 0, 4))
                with sp.Fori(0, (CHUNKS - 1) // 2) as i:
                    for j in range(2):
                        m = n + 2 + 3 * j
                        fill(layer, m, gate_up(wg, wu, layer, 2 * i + (j + 1), 0), i * 12)
                        fill(layer, m + 1, gate_up(wg, wu, layer, 2 * i + (j + 1), 4), i * 12)
                        fill(layer, m + 2, down(wd, layer, 2 * i + j), i * 12)
                fill(layer, n + FFN_PAIRS // 2 - 1, down(wd, layer, CHUNKS - 1))

            sp.dma_start(gain_rows[48:50, :], a["diff_subln"]).then_inc(rows_loaded, 16)
            sp.dma_start(x[:, 0], a["x"][0, 0:P, :]).then_inc(x_loaded, 16)
            sp.dma_start(x[:, 1], a["x"][0, P:S, :]).then_inc(x_loaded, 16)
            with sp.Fori(0, DEPTH) as layer:
                ffn(layer, 0, a["ffn1_w_gate"], a["ffn1_w_up"], a["ffn1_w_down"])
                n = MIX0 // 2
                for c0, width in PROJ:
                    if width == 512:
                        fill(layer, n, proj(layer, c0, width, 0, 4))
                        fill(layer, n + 1, proj(layer, c0, width, 4, 4))
                        n += 2
                    else:
                        fill(layer, n, proj(layer, c0, width, 0, 8))
                        n += 1
                for w, k0 in ((a["w_branch_c"], 0), (a["w_branch_c"], 2), (a["w_branch_a"], 0), (a["w_branch_b"], 0),
                              (a["w_out"], 0), (a["w_out"], 2), (a["w_out"], 4), (a["w_out"], 6)):
                    fill(layer, n, wide(w, layer, k0))
                    n += 1
                ffn(layer, FFN2_0, a["ffn2_w_gate"], a["ffn2_w_up"], a["ffn2_w_down"])
            for n, (half, cols) in enumerate(QUARTERS):
                columns = slice(512 * cols, 512 * cols + 512)
                sp.wait_ge(sem["residual_done"], DEPTH * PER_LAYER["residual_done"] + n + 1)
                sp.dma_start(a["out"][0, half * P:half * P + P, columns], x[:, half, columns]).then_inc(stored, 16)
            sp.wait_ge(stored, 16 * 4)

        PROJ_END = np.cumsum([width // 128 for _, width in PROJ]) - 1
        ROPE_CHUNKS = {0: 1, 1: 2, 3: 3, 4: 4, 5: 5}
        SQUARES_AT = {0: 9, 1: 13, 3: 21, 4: 28, 5: 32}
        ROPE_AT = {0: 10, 1: 14, 3: 22, 4: 29, 5: 33}
        SIGMOID_AT = {6: 44, 7: 45, 8: 46, 9: 47}
        SUBLN_AT = 35
        LAMBDA_AT = 15
        MERGE_C_AT, MERGE_A_AT, MERGE_B_AT, MERGED_HIGH_AT = 54, 56, 56, 58
        ROPE_HEADS = {0: (0, 8, 0, [(0, 8, True)]), 1: (1, 8, 8, [(1, 8, False)]), 3: (0, 8, 16, [(2, 4, True), (3, 4, False)]),
                      4: (1, 4, 24, [(4, 4, True)]), 5: (0, 2, 28, [(5, 2, False)])}

        def query_scale(u, t, half):
            h = {"C": 2 * u + t, "A": 16 + 2 * (u - 4) + t, "B": 24 + (u - 6) + 2 * t}[UNITS[u][0]]
            return head_scale[:, half, h:h + 1]

        def context_column(u, t):
            return {"C": 512 + P * u, "A": (2 * (u - 4) + t) * DH, "B": 256 + (u - 6 + 2 * t) * DH}[UNITS[u][0]]

        def first_guess(dve, total, n, count):
            v, guess, bits = (small[:, k, 0:n] for k in (2, 3, 4))
            dve.tensor_scalar(v, total, 1.0 / count, EPS, ALU.mult, ALU.add)
            dve.drain()
            dve.tensor_scalar(bits.bitcast(I32), v.bitcast(I32), 1, None, ALU.logical_shift_right)
            dve.drain()
            return dve.tensor_scalar(guess.bitcast(I32), bits.bitcast(I32), -1.0, float(0x5F3759DF), ALU.mult, ALU.add)

        def rotate(eng, chunk, halves):
            buf, _, scale0, parts = ROPE_HEADS[chunk]
            nh = halves.stop - halves.start
            h = DH // 2
            c0 = 0
            for table, count, is_q in parts:
                v = qk_raw[buf][:, halves, c0 * DH:(c0 + count) * DH].rearrange("p t (h d) -> p t h d", d=DH)
                w = scratch[:, halves, c0 * DH:(c0 + count) * DH].rearrange("p t (h d) -> p t h d", d=DH)
                if not is_q:
                    r = head_scale[:, halves, scale0 + c0:scale0 + c0 + count]
                    eng.tensor_tensor(v, v, r.unsqueeze(3).to_broadcast([P, nh, count, DH]), ALU.mult)
                    eng.drain()
                for to, of in ((slice(0, h), slice(h, DH)), (slice(h, DH), slice(0, h))):
                    eng.tensor_tensor(w[:, :, :, to], v[:, :, :, of],
                                      rope_sin[:, table, halves, to].unsqueeze(2).to_broadcast([P, nh, count, h]), ALU.mult)
                eng.drain()
                eng.tensor_tensor(v, v, rope_cos[:, table, halves].unsqueeze(2).to_broadcast([P, nh, count, DH]), ALU.mult)
                c0 += count
            eng.drain()

        def add_rotated(eng, chunk, halves):
            buf, heads, _, _ = ROPE_HEADS[chunk]
            if chunk == 4:
                for half in range(HALVES):
                    out = roped[:, half, P:P + 4 * DH].rearrange("p (b a d) -> p a b d", b=2, a=2)
                    v, w = (t[:, half, 0:4 * DH].rearrange("p (a b d) -> p a b d", a=2, b=2) for t in (qk_raw[buf], scratch))
                    last = eng.tensor_tensor(out, v, w, ALU.add)
                return last
            out0 = P + 4 * DH if chunk == 5 else 0
            return eng.tensor_tensor(roped[:, halves, out0:out0 + heads * DH], qk_raw[buf][:, halves, 0:heads * DH],
                                     scratch[:, halves, 0:heads * DH], ALU.add)

        @block.gpsimd
        def _(pool):
            pool.memset(ident[:, :], 0.0)
            pool.memset(masks[:, :, :], 0.0)
            pool.memset(zero[:, :].bitcast(F32), 0.0)
            pool.drain()
            pool.affine_select(out=ident[:, :], in_=ident[:, :], compare_op=ALU.not_equal, fill=1.0, base=0,
                               pattern=[[-1, P]], channel_multiplier=1)
            for n in (1, 3):
                pool.affine_select(out=masks[:, n], in_=masks[:, n], compare_op=ALU.is_ge, fill=NEG, base=0,
                                   pattern=[[-1, P]], channel_multiplier=1)
            pool.affine_select(out=masks[:, 2], in_=masks[:, 2], compare_op=ALU.is_gt, fill=NEG, base=0,
                               pattern=[[1, P]], channel_multiplier=-1)
            pool.drain().then_inc(constants_ready, 1)
            for l in range(DEPTH):
                pool.memset(gains_all[:, l, LAM_INIT_AT:LAM_INIT_AT + 1], LAM_INIT[l])
            pool.drain().then_inc(lam_init_ready, 1)
            pool.dma_start(trig[:, :, :, :], a["trig"]).then_inc(trig_loaded, 16)

            def norm(layer, n):
                v, guess, a0, b0 = (small[:, k, 0:HALVES] for k in (2, 3, 4, 5))
                pool.wait_ge(sem["norm_guessed"], value("norm_guessed", layer, n))
                for step in range(3):
                    pool.tensor_tensor(a0, guess, guess, ALU.mult)
                    pool.drain()
                    pool.tensor_tensor(b0, a0, v, ALU.mult)
                    pool.drain()
                    pool.tensor_scalar(a0, b0, -0.5, 1.5, ALU.mult, ALU.add)
                    pool.drain()
                    last = pool.tensor_tensor(norm_scale if step == 2 else guess, guess, a0, ALU.mult)
                    if step < 2:
                        pool.drain()
                last.then_inc(sem["norm_ready"], 1)

            with pool.Fori(0, DEPTH) as layer:
                norm(layer, 1)
                for i, name in enumerate(("diff_q_norm", "diff_k_norm", "moba_q_norm", "moba_k_norm", "swa_q_norm", "swa_k_norm",
                                          "diff_lambda_q1", "diff_lambda_k1", "diff_lambda_q2", "diff_lambda_k2", "swa_sinks")):
                    n = DH * i
                    pool.dma_start(params[:, n:min(n + DH, PARAMS)], a[name][bass.ds(layer, 1)].to_broadcast([P, min(DH, PARAMS - n)])
                                   ).then_inc(params_loaded, 16)
                pool.wait_ge(trig_loaded, 16)
                pool.wait_ge(params_loaded, layer * (16 * 11) + 16 * 11)
                g = params[:, ROPE_GAIN:LAM_VEC].rearrange("p (i d) -> p i d", i=6)
                shape = [P, 6, HALVES, DH]
                pool.tensor_tensor(rope_cos[:, :, :, :], g.unsqueeze(2).to_broadcast(shape),
                                   trig[:, 0].unsqueeze(1).to_broadcast(shape), ALU.mult)
                h = DH // 2
                for to, of in ((slice(0, h), slice(h, DH)), (slice(h, DH), slice(0, h))):
                    pool.tensor_tensor(rope_sin[:, :, :, to], g[:, :, of].unsqueeze(2).to_broadcast([P, 6, HALVES, h]),
                                       trig[:, 1, :, to].unsqueeze(1).to_broadcast([P, 6, HALVES, h]), ALU.mult)
                pool.drain().then_inc(sem["tables_ready"], 1)
                norm(layer, 2)
                for n, chunk in enumerate((0, 1, 3, 4, 5)):
                    halves = slice(1, 2) if chunk < 2 else slice(0, 2)
                    pool.wait_ge(sem["heads_scaled"], value("heads_scaled", layer, n + 1))
                    rotate(pool, chunk, halves)
                    if 0 < n < 4:
                        pool.wait_ge(sem["rope_turned"], value("rope_turned", layer, n))
                    add_rotated(pool, chunk, halves).then_inc(sem["rope_done"], 1)
                for n in range(4):
                    pool.wait_ge(sem["a_gated"], value("a_gated", layer, n + 1))
                    pool.tensor_tensor(merged_quarter(n), merged_quarter(n), gated(n), ALU.add
                                       ).then_inc(sem["a_added"], 1)
                norm(layer, 3)

        @block.tensor
        def _(pe):
            def three_passes(out, left_high, left_low, slot, cols, start, stop, release=0):
                first = nc.tensor.matmul(out, left_high, w_high[:, slot, cols], start=start, stop=False)
                if release:
                    first.then_inc(sem["pair_used"], release)
                nc.tensor.matmul(out, left_low, w_high[:, slot, cols], start=False, stop=False)
                return nc.tensor.matmul(out, left_high, w_low[:, slot, cols], start=False, stop=stop)

            def token(tile, kb, half):
                return tile[:, kb, half * P:(half + 1) * P]

            def turn_group(layer, stage, group, source):
                blocks = group_blocks(stage, group)
                for n, kb in enumerate(blocks):
                    for half in range(HALVES):
                        last = nc.tensor.transpose(
                            bank[GROUP_BANKS[stage][n // 2]][:, (n % 2) * S + half * P:(n % 2) * S + half * P + P],
                            source[:, half, kb * P:(kb + 1) * P], ident[:, :])
                last.then_inc(sem["blocks_turned"], 1)

            def gate_up_pair(layer, p, j, odd, i_pairs=0, release=0):
                pe.wait_ge(sem["low_ready"], value("low_ready", layer, i_pairs + p + 1))
                for k in (2 * j, 2 * j + 1):
                    for half in range(HALVES):
                        last = three_passes(bank[2 * odd + half][:, :], token(xT_high, k, half), token(xT_low, k, half), PAIR_SLOT[p],
                                            slice((k % 2) * 512, (k % 2) * 512 + 512), k == 0, k == KB - 1, release)
                        release = 0
                last.then_inc(sem["gate_up_done" if j == 3 else "pair_used"], 1)

            def wide_pair(layer, p, high, low, kb, start, i_pairs=0, release=0, before=None):
                pe.wait_ge(sem["low_ready"], value("low_ready", layer, i_pairs + p + 1))
                for n, (half, cols) in enumerate(QUARTERS):
                    if before:
                        before(n)
                    last = three_passes(quarter(half, cols)[:, :], token(high, kb, half), token(low, kb, half), PAIR_SLOT[p],
                                        slice(cols * 512, cols * 512 + 512), start, False, release)
                    release = 0
                last.then_inc(sem["pair_used"], 1)

            def last_pairs(layer, p, high, low, kb, start, before_last=None, before=None, block=None, release=0, banks=quarter):
                pe.wait_ge(sem["low_ready"], value("low_ready", layer, p + 2))
                for n, (half, cols) in enumerate(QUARTERS):
                    if before:
                        before(n)
                    if n == 3 and before_last:
                        before_last()
                    for k in range(2):
                        if block and n == 0:
                            block(k)
                        last = three_passes(banks(half, cols)[:, :], token(high, kb + k, half), token(low, kb + k, half),
                                            PAIR_SLOT[p + k], slice(cols * 512, cols * 512 + 512), start and k == 0, k == 1,
                                            release)
                        release = 0
                    last.then_inc(sem["product_done"], 1)

            def turn_hidden(layer, chunk, banks):
                pe.wait_ge(sem["hidden_ready"], value("hidden_ready", layer, chunk))
                for fb, to in enumerate(hidden_blocks(banks)):
                    for half in range(HALVES):
                        last = nc.tensor.transpose(to[:, half * P:half * P + P],
                                                   hidden[:, half, fb * P:(fb + 1) * P], ident[:, :])
                    last.then_inc(sem["hidden_turned"], 1)

            def open_quarter(n, stop=False):
                return nc.tensor.matmul(quarter(*QUARTERS[n])[:, :].rearrange("p (a b) -> p a b", a=4), zero[:, :],
                                        zero[:, :].unsqueeze(1).to_broadcast([P, 4, P]), start=True, stop=stop)

            def ffn(layer, first, stage, turned, chunks_before, after):
                if not turned:
                    pe.wait_ge(sem["residual_done"], value("residual_done", layer, -2))
                    turn_group(layer, stage, 0, x)
                pe.wait_ge(sem["blocks_low"], value("blocks_low", layer, banks_split(stage, 0, 0)))
                gate_up_pair(layer, first, 0, 0, release=2 if turned else 0)
                pe.wait_ge(sem["residual_done"], value("residual_done", layer, 0 if stage == ST_FFN1 else 8))
                pe.wait_ge(sem["blocks_low"], value("blocks_low", layer, banks_split(stage, 0, 1)))
                turn_group(layer, stage, 1, x)
                for n in range(3):
                    open_quarter(n)
                gate_up_pair(layer, first + 1, 1, 0)
                pe.wait_ge(sem["blocks_low"], value("blocks_low", layer, banks_split(stage, 1, 0)))
                gate_up_pair(layer, first + 2, 2, 0)
                pe.wait_ge(sem["blocks_low"], value("blocks_low", layer, banks_split(stage, 1, 1)))
                gate_up_pair(layer, first + 3, 3, 0)
                open_quarter(3).then_inc(sem["pair_used"], 1)
                with pe.Fori(0, (CHUNKS - 1) // 2) as i:
                    for j in range(2):
                        p = first + 4 + 6 * j
                        done = i * 2 + (chunks_before + 1 + j)
                        for n in range(4):
                            if n == HIDDEN_TURN:
                                turn_hidden(layer, done, (2 * j, 2 * j))
                            gate_up_pair(layer, p + n, n, 1 - j, i * 12)
                        pe.wait_ge(sem["hidden_low"], value("hidden_low", layer, 2 * done))
                        for n in range(2):
                            wide_pair(layer, p + 4 + n, hT_high, hT_low, n, False, i * 12, release=1 - n)
                done = chunks_before + CHUNKS
                turn_hidden(layer, done, (0, 1))

                def hidden_block(k):
                    pe.wait_ge(sem["hidden_low"], value("hidden_low", layer, 2 * done - 1 + k))

                last_pairs(layer, first + FFN_PAIRS - 2, hT_high, hT_low, 0, False, after, block=hidden_block)
                if after is None:
                    nc.tensor.matmul(bank[0][:, 0:P], zero[:, :], zero[:, :], start=True, stop=True).then_inc(sem["pair_used"], 2)

            def proj_pair(layer, chunk, j, release):
                p = MIX0 + sum(width // 128 for _, width in PROJ[:chunk]) + j
                width = PROJ[chunk][1]
                per_pair = 1024 // width
                pe.wait_ge(sem["low_ready"], value("low_ready", layer, p + 1))
                for n in range(per_pair):
                    k = j * per_pair + n
                    for half in range(HALVES):
                        last = three_passes(bank[2 * (chunk % 2) + half][:, 0:width], token(xT_high, k, half),
                                            token(xT_low, k, half), PAIR_SLOT[p], slice(n * width, (n + 1) * width),
                                            k == 0, k == KB - 1, release)
                        release = 0
                last.then_inc(sem["proj_done" if k == KB - 1 else "pair_used"], 1)

            def rope_turn(layer, n):
                first, count, _ = ROPE_TURNS[n]
                pe.wait_ge(sem["rope_done"], value("rope_done", layer, (2, 4, 5, 7)[n]))
                if n > 0:
                    pe.wait_ge(sem["rope_copied"], value("rope_copied", layer, n))
                if n >= 2:
                    pe.wait_ge(sem["context_read"], value("context_read", layer, {2: 2, 3: 4}[n]))
                for b in range(count):
                    for half in range(HALVES):
                        last = nc.tensor.transpose(bank[6 + b // 2][:, (b % 2) * S + half * P:(b % 2) * S + half * P + P],
                                                   roped[:, half, (b + (n == 3)) * P:(b + (n == 3) + 1) * P], ident[:, :])
                last.then_inc(sem["rope_turned"], 1)

            def scores(layer, u):
                kind, qb, kb, _ = UNITS[u]
                pe.wait_ge(sem["rope_copied"], value("rope_copied", layer, {"C": 2, "A": 3, "B": 4}[kind]))
                if u > 0:
                    pe.wait_ge(sem["scores_masked"], value("scores_masked", layer, u))
                else:
                    pe.wait_ge(sem["residual_done"], value("residual_done", layer, 4))
                q32, k32 = qk_blocks(qb, 1), qk_blocks(kb, 1)
                for t in range(2):
                    rows = slice(DH * t, DH * t + DH)
                    nc.tensor.matmul(bank[4 + t][:, 0:P], q32[rows, 0:P], k32[rows, 0:P], start=True, stop=True)
                    last = nc.tensor.matmul(bank[4 + t][:, P:3 * P], q32[rows, P:S], k32[rows, :], start=True, stop=True)
                last.then_inc(sem["scores_done"], 1)

            def turn_probs(layer, u):
                kind = UNITS[u][0]
                pe.wait_ge(sem["probs_ready"], value("probs_ready", layer, u + 1))
                if u > 0:
                    pe.wait_ge(sem["context_read"], value("context_read", layer, u))
                if u == 6:
                    pe.wait_ge(sem["blocks_low"], value("blocks_low", layer, banks_split(ST_O, 0, 1)))
                pe.wait_ge(sem["rope_copied"], value("rope_copied", layer, sum(pos < UNITS[u][3] + TURN_AFTER for _, _, pos in ROPE_TURNS)))
                for t in range(1 if kind == "C" else 2):
                    for b in range(3):
                        last = nc.tensor.transpose(bank[6 + t][:, b * P:(b + 1) * P], probs_of[u % 2][:, t, b * P:(b + 1) * P], ident[:, :])
                last.then_inc(sem["probs_turned"], 1)

            def context(layer, u):
                kind = UNITS[u][0]
                pe.wait_ge(sem["probs_copied"], value("probs_copied", layer, u + 1))
                for t in range(1 if kind == "C" else 2):
                    if kind == "C":
                        out, c0, dv = bank[7][:, 0:S], 384 + u * P, P
                    else:
                        out, dv = bank[6 + t][:, 384:512], DH
                        c0 = (2 * (u - 4) + t) * DH if kind == "A" else 256 + t * DH
                    pT, v = probsT[:, t], values[:, :, c0:c0 + dv]
                    nc.tensor.matmul(out[:, 0:dv], pT[:, 0:P], v[:, 0], start=True, stop=True)
                    nc.tensor.matmul(out[:, dv:2 * dv], pT[:, P:2 * P], v[:, 0], start=True, stop=False)
                    last = nc.tensor.matmul(out[:, dv:2 * dv], pT[:, 2 * P:3 * P], v[:, 1], start=False, stop=True)
                last.then_inc(sem["context_done"], 1)

            def mixing(layer):
                chunk, j = 0, 0
                for m in range(PROJ_PAIRS):
                    if m == 1:
                        pe.wait_ge(sem["residual_done"], value("residual_done", layer, 4))
                        pe.wait_ge(sem["blocks_low"], value("blocks_low", layer, banks_split(ST_MIX, 0, 1)))
                        turn_group(layer, ST_MIX, 1, x)
                    if m in (0, 1):
                        pe.wait_ge(sem["blocks_low"], value("blocks_low", layer, banks_split(ST_MIX, 0, m)))
                    if m in (2, 3):
                        pe.wait_ge(sem["blocks_low"], value("blocks_low", layer, banks_split(ST_MIX, 1, m - 2)))
                    for u, (_, _, _, pos) in enumerate(UNITS):
                        if m == pos:
                            scores(layer, u)
                    for u, (_, _, _, pos) in enumerate(UNITS):
                        if m == pos + TURN_AFTER:
                            turn_probs(layer, u)
                        if m == pos + CONTEXT_AFTER:
                            context(layer, u)
                    for n, (_, _, pos) in enumerate(ROPE_TURNS):
                        if m == pos:
                            rope_turn(layer, n)
                    if m in O_TURNS:
                        group = O_TURNS.index(m)
                        if group == 0:
                            pe.wait_ge(sem["subln_ready"], value("subln_ready", layer, 1))
                            pe.wait_ge(sem["context_read"], value("context_read", layer, 6))
                        else:
                            pe.wait_ge(sem["context_read"], value("context_read", layer, 8))
                            pe.wait_ge(sem["blocks_low"], value("blocks_low", layer, banks_split(ST_O, 0, 1)))
                        turn_group(layer, ST_O, group, o_nat)
                    if j == 0 and chunk >= 2:
                        pe.wait_ge(sem["proj_read"], value("proj_read", layer, chunk - 1))
                    if j == 0 and chunk == 1:
                        pe.wait_ge(sem["blocks_low"], value("blocks_low", layer, banks_split(ST_MIX, 1, 1)))
                    proj_pair(layer, chunk, j, release=0 if j else 1 if chunk else 2)
                    j += 1
                    if j == PROJ[chunk][1] // 128:
                        chunk, j = chunk + 1, 0

            def branches(layer):
                p = BRANCH0
                pe.wait_ge(sem["scores_masked"], value("scores_masked", layer, 8))
                pe.wait_ge(sem["blocks_low"], value("blocks_low", layer, banks_split(ST_O, 1, 1)))
                for k in range(2):
                    wide_pair(layer, p + k, oT_high, oT_low, 4 + k, k == 0, release=1 - k)
                last_pairs(layer, p + 2, oT_high, oT_low, 6, False)
                pe.wait_ge(sem["proj_read"], value("proj_read", layer, len(PROJ)))
                last_pairs(layer, p + 4, oT_high, oT_low, 0, True, release=2, banks=a_quarter)

                def quarter_free(n):
                    pe.wait_ge(sem["merged"], value("merged", layer, n + 1))

                def turn_merged():
                    pe.wait_ge(sem["merged"], value("merged", layer, 6))
                    turn_group(layer, ST_MERGED, 0, merged)

                last_pairs(layer, p + 6, oT_high, oT_low, 2, True, turn_merged, quarter_free, release=2)
                p = OUT0

                def b_merged(n):
                    pe.wait_ge(sem["merged"], value("merged", layer, 5 + n))

                for k in range(KB - 2):
                    if k % 2 == 0:
                        pe.wait_ge(sem["blocks_low"], value("blocks_low", layer, banks_split(ST_MERGED, k // 4, k % 4 // 2)))
                    if k == 1:
                        pe.wait_ge(sem["blocks_low"], value("blocks_low", layer, banks_split(ST_MERGED, 0, 1)))
                        turn_group(layer, ST_MERGED, 1, merged)
                    wide_pair(layer, p + k, xT_high, xT_low, k, k == 0, release=2 if k == 0 else 0, before=b_merged if k == 0 else None)
                pe.wait_ge(sem["blocks_low"], value("blocks_low", layer, banks_split(ST_MERGED, 1, 1)))

                def turn_residual():
                    pe.wait_ge(sem["residual_done"], value("residual_done", layer, 6))
                    turn_group(layer, ST_FFN2, 0, x)

                last_pairs(layer, p + KB - 2, xT_high, xT_low, KB - 2, False, turn_residual)

            pe.sem_inc(sem["pair_used"], CREDIT["pair_used"])
            pe.wait_ge(constants_ready, 1)
            for n in range(4):
                open_quarter(n, True).then_inc(sem["product_done"], 1)
            pe.wait_ge(rows_loaded, 16 * 4)
            nc.tensor.transpose(bank[0][:, 0:GAIN_ROWS], gain_rows[0:GAIN_ROWS, :], ident[0:GAIN_ROWS, 0:GAIN_ROWS]
                                ).then_inc(gains_turned, 1)
            with pe.Fori(0, DEPTH) as layer:
                def turn_for_mixing():
                    pe.wait_ge(sem["residual_done"], value("residual_done", layer, 2))
                    turn_group(layer, ST_MIX, 0, x)

                ffn(layer, 0, ST_FFN1, False, 0, turn_for_mixing)
                mixing(layer)
                branches(layer)
                ffn(layer, FFN2_0, ST_FFN2, True, CHUNKS, None)

        @block.scalar
        def _(act):
            def high(layer, p, p_reg=None, fills=0):
                n, slot = p // 2, PAIR_SLOT[p]
                reg = 0 if p_reg is None else p_reg
                in_slot = FILL_SLOT[n]
                act.wait_ge(fill_landed[in_slot], (layer * FILL_SLOT.count(in_slot) + (FILL_SLOT[:n + 1].count(in_slot) + fills)) * 32)
                act.wait_ge(sem["pair_used"], value("pair_used", layer, reg + PAIR_BEFORE[p] + 1))
                act.activation(w_high[:, slot], raw[:, in_slot, (p % 2) * 1024:(p % 2) * 1024 + 1024], ACT.Copy
                               ).then_inc(sem["high_ready"], 1)

            def blocks_high(layer, stage, group, gain):
                tile = stage_tiles(stage)[0]
                blocks = group_blocks(stage, group)
                act.wait_ge(sem["blocks_turned"], value("blocks_turned", layer, 2 * stage + group + 1))
                for b in range(2):
                    source = bank[GROUP_BANKS[stage][b]]
                    if gain is None:
                        last = act.activation(tile[:, blocks[2 * b]:blocks[2 * b] + 2, :],
                                              source[:, :].rearrange("p (k s) -> p k s", k=2), ACT.Copy)
                    elif gain == G_SUBLN:
                        last = act.activation(tile[:, blocks[2 * b]:blocks[2 * b] + 2, :],
                                              source[:, :].rearrange("p (k s) -> p k s", k=2), ACT.Copy,
                                              scale=gains[:, gain:gain + 1])
                    else:
                        for n in range(2):
                            kb = blocks[2 * b + n]
                            last = act.activation(tile[:, kb, :], source[:, n * S:(n + 1) * S], ACT.Copy,
                                                  scale=gains[:, gain + kb:gain + kb + 1])
                    last.then_inc(sem["blocks_high"], 1)

            def norm_turned(layer, stage, gain, residuals, pairs=()):
                blocks_high(layer, stage, 0, gain)
                for p in pairs[:2]:
                    high(layer, p)
                if pairs:
                    blocks_high(layer, stage, 1, gain)
                act.wait_ge(sem["residual_done"], value("residual_done", layer, residuals))
                for half in range(HALVES):
                    last = act.activation(scratch[:, :, :].rearrange("p t c -> p (t c)"), x[:, half], ACT.Square,
                                          accum_out=norm_sq[:, half:half + 1])
                    if half == 0:
                        act.drain()
                last.then_inc(sem["squares_ready"], 1)
                if not pairs:
                    blocks_high(layer, stage, 1, gain)
                for p in pairs[2:]:
                    high(layer, p)

            def silu_gate(layer, chunk, odd, norm):
                act.wait_ge(sem["gate_up_done"], value("gate_up_done", layer, chunk))
                act.wait_ge(sem["norm_ready"], value("norm_ready", layer, norm))
                for half in range(HALVES):
                    act.activation(silu[:, half], bank[2 * odd + half][:, 0:FC], ACT.Silu, scale=norm_scale[:, half:half + 1]
                                   ).then_inc(sem["silu_ready"], 1)

            def hidden_high(layer, chunk, odd):
                act.wait_ge(sem["hidden_turned"], value("hidden_turned", layer, 2 * chunk))
                act.activation(hT_high[:, :, :], bank[2 * odd][:, :].rearrange("p (k s) -> p k s", k=2), ACT.Copy
                               ).then_inc(sem["hidden_high"], 2)

            def last_hidden_high(layer, chunk):
                for fb, source in enumerate(hidden_blocks((0, 1))):
                    act.wait_ge(sem["hidden_turned"], value("hidden_turned", layer, 2 * chunk - 1 + fb))
                    act.activation(hT_high[:, fb], source, ACT.Copy).then_inc(sem["hidden_high"], 1)

            def ffn_chunks(layer, first, before):
                act.activation(sink_exp_of[0][:, 0:1], zero[:, 0:1].bitcast(F32), ACT.Silu)
                act.drain()
                with act.Fori(0, (CHUNKS - 1) // 2) as i:
                    for j in range(2):
                        p = first + 4 + 6 * j
                        for n in range(6):
                            if n == SILU_AT:
                                silu_gate(layer, i * 2 + (before + 1 + j), j, 3 if before else 1)
                            high(layer, p + n, i * 12, i)
                        hidden_high(layer, i * 2 + (before + 1 + j), j)

            def last_chunk(layer, first, before, following):
                p = first + FFN_PAIRS - 2
                high(layer, p)
                high(layer, p + 1)
                if following:
                    high(layer, p + 2)
                silu_gate(layer, before + CHUNKS, 0, 3 if before else 1)
                if following:
                    high(layer, p + 3)
                last_hidden_high(layer, before + CHUNKS)
                if following:
                    high(layer, p + 4)
                    high(layer, p + 5)

            def read_proj(layer, chunk):
                act.wait_ge(sem["proj_done"], value("proj_done", layer, chunk + 1))
                if chunk == 0:
                    act.wait_ge(sem["norm_ready"], value("norm_ready", layer, 2))
                done = {3: 2, 4: 4, 5: 5}.get(chunk)
                if done:
                    act.wait_ge(sem["rope_done"], value("rope_done", layer, done))
                for half in range(HALVES):
                    source, scale = bank[2 * (chunk % 2) + half], norm_scale[:, half:half + 1]
                    if chunk >= 6:
                        c0 = 512 * (chunk - 6)
                        last = act.activation(gates[:, half, c0:c0 + 512], source[:, :],
                                              ACT.Copy if chunk in SIGMOID_AT else ACT.Sigmoid, scale=scale)
                        continue
                    parts = {0: [(qk_raw[0], 0, 0, 512)], 1: [(qk_raw[1], 0, 0, 512)], 2: [(values, 384, 0, 512)],
                             3: [(qk_raw[0], 0, 0, 512)], 4: [(values, 0, 0, 256), (qk_raw[1], 0, 256, 256)],
                             5: [(qk_raw[0], 0, 0, 128), (values, 256, 128, 128)]}[chunk]
                    for tile, to, c0, width in parts:
                        last = act.activation(tile[:, half, to:to + width], source[:, c0:c0 + width], ACT.Copy, scale=scale)
                last.then_inc(sem["proj_read"], 1)

            def head_squares(layer, chunk):
                buf, heads, _, _ = ROPE_HEADS[chunk]
                act.drain()
                if chunk:
                    act.wait_ge(sem["rope_done"], value("rope_done", layer, {1: 2, 3: 4, 4: 5, 5: 6}[chunk]))
                act.activation(scratch[:, :, 0:heads * DH], qk_raw[buf][:, :, 0:heads * DH], ACT.Square
                               ).then_inc(sem["head_squares"], 1)

            def copy_rope(layer, n):
                first, count, _ = ROPE_TURNS[n]
                act.wait_ge(sem["rope_turned"], value("rope_turned", layer, n + 1))
                for b in range(0, count, 2):
                    w = min(2, count - b)
                    last = act.activation(qk_blocks(first + b, w), bank[6 + b // 2][:, 0:w * S], ACT.Copy)
                last.then_inc(sem["rope_copied"], 1)

            def exps(layer, u):
                probs, neg_max, row_sum = probs_of[u % 2], neg_max_of[u % 2], row_sum_of[u % 2]
                act.wait_ge(sem["scores_masked"], value("scores_masked", layer, u + 1))
                for t in range(2):
                    for half, cols in ((0, slice(0, P)), (1, slice(P, 3 * P))):
                        n = 2 * t + half
                        last = act.activation(probs[:, t, cols], probs[:, t, cols], ACT.Exp, bias=neg_max[:, n:n + 1],
                                              accum_out=row_sum[:, n:n + 1])
                if UNITS[u][0] == "B":
                    last = act.activation(sink_exp_of[u % 2][:, :], sink_diff_of[u % 2][:, :], ACT.Exp)
                last.then_inc(sem["exps_ready"], 1)

            def copy_probs(layer, u):
                act.wait_ge(sem["probs_turned"], value("probs_turned", layer, u + 1))
                for t in range(1 if UNITS[u][0] == "C" else 2):
                    last = act.activation(probsT[:, t], bank[6 + t][:, 0:3 * P], ACT.Copy)
                last.then_inc(sem["probs_copied"], 1)

            def read_context(layer, u):
                act.wait_ge(sem["context_done"], value("context_done", layer, u + 1))
                if UNITS[u][0] == "C":
                    c0 = context_column(u, 0)
                    last = act.activation(o_nat[:, :, c0:c0 + P], bank[7][:, 0:S].rearrange("p (t c) -> p t c", t=2), ACT.Copy)
                else:
                    for t in range(2):
                        c0 = context_column(u, t)
                        for half in range(HALVES):
                            last = act.activation(o_nat[:, half, c0:c0 + DH], bank[6 + t][:, 384 + half * DH:384 + half * DH + DH],
                                                  ACT.Copy, scale=inv_sum_of[u % 2][:, 2 * t + half:2 * t + half + 1])
                last.then_inc(sem["context_read"], 1)

            def mixing(layer):
                norm_turned(layer, ST_MIX, G_MIX, 4)
                for m in range(4, FFN2_0 - MIX0 + 4):
                    for chunk, end in enumerate(PROJ_END):
                        if m == end + RING:
                            read_proj(layer, chunk)
                    if m == LAMBDA_AT:
                        act.wait_ge(sem["lambda_sums"], value("lambda_sums", layer, 1))
                        act.activation(small[:, 1, 0:2], small[:, 0, 0:2], ACT.Exp).then_inc(sem["lambda_exps"], 1)
                    for n, (_, _, pos) in enumerate(ROPE_TURNS):
                        if m == pos + RING - 1:
                            copy_rope(layer, n)
                    for u, (_, _, _, pos) in enumerate(UNITS):
                        if m == pos + TURN_AFTER + RING - 1:
                            copy_probs(layer, u)
                        if m == pos + CONTEXT_AFTER + RING - 1:
                            read_context(layer, u)
                    for u, (_, _, _, pos) in enumerate(UNITS):
                        if m == pos + RING:
                            exps(layer, u)
                    for chunk, at in SQUARES_AT.items():
                        if m == at:
                            head_squares(layer, chunk)
                    if m == SUBLN_AT:
                        act.drain()
                        act.wait_ge(sem["rope_done"], value("rope_done", layer, 7))
                        act.activation(scratch[:, :, :], o_nat[:, :, 512:1024], ACT.Square).then_inc(sem["subln_squares"], 1)
                    for group, pos in enumerate(O_TURNS):
                        if m == pos + RING - 1:
                            blocks_high(layer, ST_O, group, None if group else G_SUBLN)
                    for chunk, at in SIGMOID_AT.items():
                        if m == at:
                            v = gates[:, :, 512 * (chunk - 6):512 * (chunk - 5)]
                            act.drain()
                            act.activation(v, v, ACT.Sigmoid)
                    if m == MERGED_HIGH_AT:
                        blocks_high(layer, ST_MERGED, 0, None)
                        blocks_high(layer, ST_MERGED, 1, None)
                    high(layer, MIX0 + m)

            for n, name in enumerate(("ffn1_norm", "mix_norm", "ffn2_norm")):
                act.dma_start(gain_rows[16 * n:16 * n + 16, :], a[name].rearrange("l (k p) -> (l k) p", p=P)).then_inc(rows_loaded, 16)
            act.wait_ge(gains_turned, 1)
            for i, g in enumerate((G_FFN1, G_MIX, G_FFN2)):
                act.activation(gains_all[:, :, g:g + KB], bank[0][:, 16 * i:16 * i + 16].rearrange("p (l k) -> p l k", l=DEPTH), ACT.Copy)
            for l in range(DEPTH):
                act.activation(gains_all[:, l, G_SUBLN:G_SUBLN + 1], bank[0][:, 48 + l:49 + l], ACT.Copy, scale=1.0 - LAM_INIT[l])
            act.drain().then_inc(gains_ready, 1)
            act.wait_ge(constants_ready, 1)
            with act.Fori(0, DEPTH) as layer:
                act.activation(sink_exp_of[0][:, 0:1], zero[:, 0:1].bitcast(F32), ACT.Copy)
                high(layer, 0)
                act.wait_ge(sem["gains_copied"], value("gains_copied", layer, 1))
                norm_turned(layer, ST_FFN1, G_FFN1, 0, (1, 2, 3))
                ffn_chunks(layer, 0, 0)
                last_chunk(layer, 0, 0, True)
                mixing(layer)
                norm_turned(layer, ST_FFN2, G_FFN2, 8)
                ffn_chunks(layer, FFN2_0, CHUNKS)
                last_chunk(layer, FFN2_0, CHUNKS, False)

        @block.vector
        def _(dve):
            def low(layer, p, p_reg=None):
                slot = PAIR_SLOT[p]
                reg = 0 if p_reg is None else p_reg
                dve.wait_ge(sem["high_ready"], value("high_ready", layer, reg + p + 1))
                dve.tensor_tensor(w_low[:, slot], raw[:, FILL_SLOT[p // 2], (p % 2) * 1024:(p % 2) * 1024 + 1024],
                                  w_high[:, slot].bitcast(F32), ALU.subtract).then_inc(sem["low_ready"], 1)

            def blocks_low(layer, stage, group, gain):
                high_tile, low_tile = stage_tiles(stage)
                blocks = group_blocks(stage, group)
                for b in range(2):
                    source = bank[GROUP_BANKS[stage][b]]
                    dve.wait_ge(sem["blocks_high"], value("blocks_high", layer, 4 * stage + 2 * group + b + 1))
                    if gain is None or gain == G_SUBLN:
                        kb = blocks[2 * b]
                        last = dve.scalar_tensor_tensor(
                            low_tile[:, kb:kb + 2, :], source[:, :].rearrange("p (k s) -> p k s", k=2),
                            1.0 if gain is None else gains[:, gain:gain + 1], high_tile[:, kb:kb + 2, :].bitcast(F32),
                            ALU.mult, ALU.subtract)
                    else:
                        for n in range(2):
                            kb = blocks[2 * b + n]
                            last = dve.scalar_tensor_tensor(
                                low_tile[:, kb, :], source[:, n * S:(n + 1) * S], gains[:, gain + kb:gain + kb + 1],
                                high_tile[:, kb, :].bitcast(F32), ALU.mult, ALU.subtract)
                    last.then_inc(sem["blocks_low"], 1)

            def residual(layer, n, product, factor):
                half, cols = QUARTERS[n]
                dve.wait_ge(sem["product_done"], value("product_done", layer, product + n + 1))
                v = x[:, half, 512 * cols:512 * cols + 512]
                dve.scalar_tensor_tensor(v, quarter(half, cols)[:, :], factor, v, ALU.mult, ALU.add
                                         ).then_inc(sem["residual_done"], 1)

            def inverse_root(out, total, n, shape, count):
                v, guess, a0, b0 = (small[:, k, 0:n] for k in (2, 3, 4, 5))
                first_guess(dve, total, n, count)
                dve.drain()
                for step in range(3):
                    dve.tensor_tensor(a0, guess, guess, ALU.mult)
                    dve.drain()
                    dve.scalar_tensor_tensor(b0, a0, -0.5, v, ALU.mult, ALU.mult)
                    dve.drain()
                    if step < 2:
                        dve.scalar_tensor_tensor(guess, b0, 1.5, guess, ALU.add, ALU.mult)
                        dve.drain()
                return dve.scalar_tensor_tensor(out, shape(b0), 1.5, shape(guess), ALU.add, ALU.mult)

            def norm_guess(layer, n):
                dve.wait_ge(sem["squares_ready"], value("squares_ready", layer, n))
                first_guess(dve, norm_sq, HALVES, D).then_inc(sem["norm_guessed"], 1)

            def multiply_hidden(layer, chunk, odd):
                for half in range(HALVES):
                    dve.wait_ge(sem["silu_ready"], value("silu_ready", layer, 2 * chunk + (half - 1)))
                    last = dve.scalar_tensor_tensor(hidden[:, half], bank[2 * odd + half][:, FC:2 * FC], norm_scale[:, half:half + 1],
                                                    silu[:, half], ALU.mult, ALU.mult)
                last.then_inc(sem["hidden_ready"], 1)

            def hidden_low(layer, chunk, odd):
                dve.wait_ge(sem["hidden_high"], value("hidden_high", layer, 2 * chunk))
                dve.tensor_tensor(hT_low[:, :, :], bank[2 * odd][:, :].rearrange("p (k s) -> p k s", k=2),
                                  hT_high[:, :, :].bitcast(F32), ALU.subtract).then_inc(sem["hidden_low"], 2)

            def last_hidden_low(layer, chunk):
                for fb, source in enumerate(hidden_blocks((0, 1))):
                    dve.wait_ge(sem["hidden_high"], value("hidden_high", layer, 2 * chunk - 1 + fb))
                    dve.tensor_tensor(hT_low[:, fb], source, hT_high[:, fb].bitcast(F32), ALU.subtract
                                      ).then_inc(sem["hidden_low"], 1)

            def ffn_chunks(layer, first, before):
                with dve.Fori(0, (CHUNKS - 1) // 2) as i:
                    for j in range(2):
                        p = first + 4 + 6 * j
                        for n in range(6):
                            if n == SILU_AT:
                                multiply_hidden(layer, i * 2 + (before + 1 + j), j)
                            low(layer, p + n, i * 12)
                        hidden_low(layer, i * 2 + (before + 1 + j), j)

            def last_chunk(layer, first, before, following):
                p = first + FFN_PAIRS - 2
                low(layer, p)
                low(layer, p + 1)
                if following:
                    low(layer, p + 2)
                multiply_hidden(layer, before + CHUNKS, 0)
                if following:
                    low(layer, p + 3)
                last_hidden_low(layer, before + CHUNKS)
                if following:
                    low(layer, p + 4)
                    low(layer, p + 5)

            def add_and_turn(layer, stage, gain, product, factor, n):
                for q in range(3):
                    residual(layer, q, product, factor)
                blocks_low(layer, stage, 0, gain)
                residual(layer, 3, product, factor)
                blocks_low(layer, stage, 1, gain)
                norm_guess(layer, n)

            def lambda_exponents(layer):
                dve.wait_ge(params_loaded, layer * (16 * 11) + 16 * 11)
                dve.sem_inc(dve_waited, 1)
                vec = params[:, LAM_VEC:SINK].rearrange("p (i d) -> p i d", i=4)
                for n in range(2):
                    dve.tensor_tensor_reduce(out=scratch[:, 0, 0:DH], in0=vec[:, 2 * n], in1=vec[:, 2 * n + 1], scale=1.0, scalar=0.0,
                                             op0=ALU.mult, op1=ALU.add, accum_out=small[:, 0, n:n + 1])
                    dve.drain()
                dve.sem_inc(sem["lambda_sums"], 1)

            def scale_heads(layer, chunk):
                _, heads, scale0, parts = ROPE_HEADS[chunk]
                total = small[:, 6, 0:HALVES * heads]
                dve.wait_ge(sem["head_squares"], value("head_squares", layer, ROPE_CHUNKS[chunk]))
                dve.tensor_reduce(total.rearrange("p (t h) -> p t h", t=HALVES),
                                  scratch[:, :, 0:heads * DH].rearrange("p t (h d) -> p t h d", d=DH), axis=AXIS_X, op=ALU.add)
                dve.drain()
                last = inverse_root(head_scale[:, :, scale0:scale0 + heads], total, HALVES * heads,
                                    lambda v: v.rearrange("p (t h) -> p t h", t=HALVES), DH)
                table, count, is_q = parts[0]
                if is_q:
                    dve.drain()
                    r = head_scale[:, :, scale0:scale0 + count]
                    last = dve.tensor_scalar(r, r, SCALE, None, ALU.mult)
                last.then_inc(sem["heads_scaled"], 1)

            def rope(layer, chunk):
                dve.drain()
                if chunk == 0:
                    dve.wait_ge(sem["tables_ready"], value("tables_ready", layer, 1))
                rotate(dve, chunk, slice(0, 1))
                if chunk == 1:
                    dve.wait_ge(sem["rope_turned"], value("rope_turned", layer, 1))
                add_rotated(dve, chunk, slice(0, 1)).then_inc(sem["rope_done"], 1)

            def mask_scores(layer, u):
                kind = UNITS[u][0]
                probs, row_max, neg_max, sink_diff = (v[u % 2] for v in (probs_of, row_max_of, neg_max_of, sink_diff_of))
                dve.wait_ge(sem["scores_done"], value("scores_done", layer, u + 1))
                if u > 1:
                    dve.wait_ge(sem["probs_turned"], value("probs_turned", layer, u - 1))
                dve.sem_inc(dve_waited, 1)
                for t in range(2):
                    for half, cols in ((0, slice(0, P)), (1, slice(P, 3 * P))):
                        mask = masks[:, 1] if half == 0 else masks[:, 2:4] if kind == "B" else masks[:, 0:2]
                        out, source = probs[:, t, cols], bank[4 + t][:, cols]
                        if half:
                            out, source = (v.rearrange("p (b k) -> p b k", b=2) for v in (out, source))
                        dve.tensor_tensor_reduce(out=out, in0=source, in1=mask, scale=query_scale(u, t, half), scalar=-3e38,
                                                 op0=ALU.add, op1=ALU.max, accum_out=row_max[:, 2 * t + half:2 * t + half + 1])
                dve.drain()
                if kind == "B":
                    for t in range(2):
                        n = SINK + (u - 6) + 2 * t
                        v = row_max[:, 2 * t:2 * t + 2]
                        dve.tensor_scalar(v, v, params[:, n:n + 1], None, ALU.max)
                    dve.drain()
                    for t in range(2):
                        n = SINK + (u - 6) + 2 * t
                        dve.tensor_scalar(sink_diff[:, 2 * t:2 * t + 2], row_max[:, 2 * t:2 * t + 2], params[:, n:n + 1], -1.0,
                                          ALU.subtract, ALU.mult)
                dve.tensor_scalar(neg_max[:, :], row_max[:, :], -1.0, None, ALU.mult).then_inc(sem["scores_masked"], 1)

            def normalise(layer, u):
                kind = UNITS[u][0]
                probs, row_sum, inv_sum, sink_exp = (v[u % 2] for v in (probs_of, row_sum_of, inv_sum_of, sink_exp_of))
                if u == 0:
                    dve.wait_ge(sem["lambda_exps"], value("lambda_exps", layer, 1))
                    dve.tensor_tensor(neg_lam[:, 1:2], small[:, 1, 1:2], gains[:, LAM_INIT_AT:LAM_INIT_AT + 1], ALU.subtract)
                    dve.drain()
                    dve.tensor_tensor(neg_lam[:, 0:1], neg_lam[:, 1:2], small[:, 1, 0:1], ALU.subtract)
                dve.wait_ge(sem["exps_ready"], value("exps_ready", layer, u + 1))
                if kind == "B":
                    dve.tensor_tensor(row_sum[:, :], row_sum[:, :], sink_exp[:, :], ALU.add)
                    dve.drain()
                last = dve.reciprocal(inv_sum[:, :], row_sum[:, :])
                if kind == "C":
                    dve.drain()
                    dve.tensor_scalar(inv_sum[:, 2:4], inv_sum[:, 2:4], neg_lam[:, 0:1], None, ALU.mult)
                    dve.drain()
                    for half, cols in ((0, slice(0, P)), (1, slice(P, 3 * P))):
                        dve.tensor_scalar(probs[:, 1, cols], probs[:, 1, cols], inv_sum[:, 2 + half:3 + half], None, ALU.mult)
                    dve.drain()
                    for half, cols in ((0, slice(0, P)), (1, slice(P, 3 * P))):
                        last = dve.scalar_tensor_tensor(probs[:, 0, cols], probs[:, 0, cols], inv_sum[:, half:half + 1],
                                                        probs[:, 1, cols], ALU.mult, ALU.add)
                last.then_inc(sem["probs_ready"], 1)

            def subln(layer):
                dve.wait_ge(sem["subln_squares"], value("subln_squares", layer, 1))
                total = small[:, 6, 0:HALVES * 4]
                dve.tensor_reduce(total.rearrange("p (t h) -> p t h", t=HALVES),
                                  scratch[:, :, :].rearrange("p t (h d) -> p t h d", d=P), axis=AXIS_X, op=ALU.add)
                dve.drain()
                scales = small[:, 7, 0:HALVES * 4]
                inverse_root(scales, total, HALVES * 4, lambda v: v, P)
                dve.drain()
                v = o_nat[:, :, 512:1024].rearrange("p t (h d) -> p t h d", d=P)
                r = scales.rearrange("p (t h) -> p t h", t=HALVES).unsqueeze(3).to_broadcast([P, HALVES, 4, P])
                dve.tensor_tensor(v, v, r, ALU.mult).then_inc(sem["subln_ready"], 1)

            def merge_c(layer):
                dve.wait_ge(sem["proj_read"], value("proj_read", layer, len(PROJ)))
                for n in range(4):
                    dve.wait_ge(sem["product_done"], value("product_done", layer, 4 + n + 1))
                    dve.tensor_tensor(merged_quarter(n), quarter(*QUARTERS[n])[:, :], gate(2, n), ALU.mult
                                      ).then_inc(sem["merged"], 1)

            def gate_a(layer):
                for n in range(4):
                    dve.wait_ge(sem["product_done"], value("product_done", layer, 8 + n + 1))
                    dve.tensor_tensor(gated(n), a_quarter(*QUARTERS[n])[:, :], gate(0, n), ALU.mult).then_inc(sem["a_gated"], 1)

            def merge_b(layer, n):
                dve.wait_ge(sem["product_done"], value("product_done", layer, 12 + n + 1))
                dve.tensor_tensor(scratch[:, n % 2], quarter(*QUARTERS[n])[:, :], gate(1, n), ALU.mult)
                dve.drain()
                dve.wait_ge(sem["a_added"], value("a_added", layer, n + 1))
                dve.tensor_tensor(merged_quarter(n), merged_quarter(n), scratch[:, n % 2], ALU.add).then_inc(sem["merged"], 1)

            def mixing(layer):
                add_and_turn(layer, ST_MIX, G_MIX, 0, 0.5, 2)
                lambda_exponents(layer)
                for m in range(4, FFN2_0 - MIX0 + 4):
                    for u, (_, _, _, pos) in enumerate(UNITS):
                        if m == pos + 6:
                            normalise(layer, u)
                    for u, (_, _, _, pos) in enumerate(UNITS):
                        if m == pos + 5:
                            mask_scores(layer, u)
                    for chunk, at in ROPE_AT.items():
                        if m == at:
                            scale_heads(layer, chunk)
                            if chunk < 3:
                                rope(layer, chunk)
                    if m == SUBLN_AT + 1:
                        subln(layer)
                    for group, pos in enumerate(O_TURNS):
                        if m == pos + RING - 1:
                            blocks_low(layer, ST_O, group, None if group else G_SUBLN)
                    if m == MERGE_C_AT:
                        merge_c(layer)
                    if m == MERGE_A_AT:
                        gate_a(layer)
                    if m == MERGE_B_AT:
                        for n in range(4):
                            if n == 3:
                                blocks_low(layer, ST_MERGED, 0, None)
                            merge_b(layer, n)
                        blocks_low(layer, ST_MERGED, 1, None)
                    low(layer, MIX0 + m)

            dve.sem_inc(sem["low_ready"], CREDIT["low_ready"])
            dve.wait_ge(x_loaded, 32)
            with dve.Fori(0, DEPTH) as layer:
                residual(layer, 0, -4, 0.5)
                residual(layer, 1, -4, 0.5)
                dve.wait_ge(gains_ready, 1)
                dve.wait_ge(lam_init_ready, 1)
                dve.tensor_copy(gains[:, :], gains_all[:, bass.ds(layer, 1), :].rearrange("p o c -> p (o c)")
                                ).then_inc(sem["gains_copied"], 1)
                low(layer, 0)
                blocks_low(layer, ST_FFN1, 0, G_FFN1)
                residual(layer, 2, -4, 0.5)
                residual(layer, 3, -4, 0.5)
                low(layer, 1)
                low(layer, 2)
                blocks_low(layer, ST_FFN1, 1, G_FFN1)
                low(layer, 3)
                norm_guess(layer, 1)
                ffn_chunks(layer, 0, 0)
                last_chunk(layer, 0, 0, True)
                mixing(layer)
                add_and_turn(layer, ST_FFN2, G_FFN2, 16, 1.0, 3)
                ffn_chunks(layer, FFN2_0, CHUNKS)
                last_chunk(layer, FFN2_0, CHUNKS, False)
            for q in range(4):
                residual(DEPTH, q, -4, 0.5)


_INS = ["x", "ffn1_norm", "ffn1_w_gate", "ffn1_w_up", "ffn1_w_down", "mix_norm", "w_in", "moba_q_norm", "moba_k_norm",
        "swa_q_norm", "swa_k_norm", "swa_sinks", "diff_q_norm", "diff_k_norm", "diff_lambda_q1", "diff_lambda_k1",
        "diff_lambda_q2", "diff_lambda_k2", "diff_subln", "w_branch_a", "w_branch_b", "w_branch_c", "w_out", "ffn2_norm",
        "ffn2_w_gate", "ffn2_w_up", "ffn2_w_down"]


def rotary_constants():
    inv_freq = np.float32(10000.0) ** (-np.arange(0, DH, 2, dtype=np.float32) / np.float32(DH))
    angle = np.arange(S, dtype=np.float32)[:, None] * inv_freq[None, :]
    cos, sin = np.cos(angle), np.sin(angle)
    table = np.stack([np.concatenate([cos, cos], 1), np.concatenate([-sin, sin], 1)])
    return np.ascontiguousarray(table.reshape(2, HALVES, P, DH).transpose(2, 0, 1, 3).astype(np.float32))


def kernel(**inputs):
    import concourse.bacc as bacc
    from concourse.bass_utils import run_bass_kernel_spmd

    nc = bacc.Bacc("TRN2", target_bir_lowering=False, num_devices=1)
    arrays = {name: np.ascontiguousarray(inputs[name]) for name in _INS}
    arrays["trig"] = rotary_constants()
    tensors = {name: nc.dram_tensor(f"in_{name}", v.shape, mybir.dt.from_np(v.dtype), kind="ExternalInput").ap()
               for name, v in arrays.items()}
    tensors["out"] = nc.dram_tensor("out", (1, S, D), F32, kind="ExternalOutput").ap()
    build(nc, tensors)
    r = run_bass_kernel_spmd(nc, [{f"in_{name}": v for name, v in arrays.items()}], core_ids=[0])
    return r.results[0]["out"]
```
